# Optimizing a Trainium2 kernel written in Bass

```python
import math
import jax
import jax.numpy as jnp
from jax import lax
import numpy as np

D_MODEL = 1024
BATCH = 1
SEQ = 1024
DEPTH = 1

HEAD_DIM = 64
N_SB_HEADS = 6
DIL_GROUPS = ((128, 1), (512, 4), (2048, 16))
HG = 2
N_DIL_HEADS = HG * len(DIL_GROUPS)
N_X_HEADS = 4
N_MEM = 256
D_FF = 2816
N_BUCKETS = 32
MAX_DISTANCE = 2048
Q_BLOCK = 128
EPS = 1e-6
N_BRANCH = 3
SB_W = N_SB_HEADS * HEAD_DIM
DIL_W = N_DIL_HEADS * HEAD_DIM
DIL_OUT_W = HG * HEAD_DIM
X_W = N_X_HEADS * HEAD_DIM
IN_COLS = 3 * SB_W + 3 * DIL_W + X_W + N_BRANCH * D_MODEL

kernel_name = "hybrid_gated_stickbreak_dilated_memory_macaron"

def _rmsnorm(x, g):
    xf = x.astype(jnp.float32)
    y = xf * lax.rsqrt(jnp.mean(xf * xf, axis=-1, keepdims=True) + EPS)
    return (y * g.astype(jnp.float32)).astype(x.dtype)

def _swiglu(h, w_gu, w_down):
    a, b = jnp.split(h @ w_gu, 2, axis=-1)
    return (jax.nn.silu(a) * b) @ w_down

def _t5_bucket(dist):
    max_exact = N_BUCKETS // 2
    nf = jnp.maximum(dist, 1).astype(jnp.float32)
    large = max_exact + (jnp.log(nf / max_exact) / math.log(MAX_DISTANCE / max_exact)
                         * (N_BUCKETS - max_exact)).astype(jnp.int32)
    large = jnp.minimum(large, N_BUCKETS - 1)
    return jnp.where(dist < max_exact, dist, large)

def _stick_breaking(q, k, v):
    B, S, H, Dh = q.shape
    scale = 1.0 / math.sqrt(Dh)
    s_pos = jnp.arange(S, dtype=jnp.int32)

    def block(t0):
        qb = lax.dynamic_slice_in_dim(q, t0, Q_BLOCK, axis=1)
        z = jnp.einsum('bqhd,bkhd->bhqk', qb, k).astype(jnp.float32) * scale
        t = t0 + jnp.arange(Q_BLOCK, dtype=jnp.int32)
        causal = (s_pos[None, :] < t[:, None])[None, None]
        log_beta = jax.nn.log_sigmoid(z)
        log_keep = jnp.where(causal, jax.nn.log_sigmoid(-z), 0.0)
        after = lax.cumsum(log_keep, axis=3, reverse=True) - log_keep
        a = jnp.where(causal, jnp.exp(log_beta + after), 0.0)
        return jnp.einsum('bhqk,bkhd->bqhd', a.astype(v.dtype), v)

    starts = jnp.arange(S // Q_BLOCK, dtype=jnp.int32) * Q_BLOCK
    o = lax.map(block, starts)
    return o.transpose(1, 0, 2, 3, 4).reshape(B, S, H * Dh)

def _dilated_attention(q, k, v, rel_bias):
    B, S, _, Dh = q.shape
    qs = [q[:, :, g * HG:(g + 1) * HG] for g in range(len(DIL_GROUPS))]
    ks = [k[:, :, g * HG:(g + 1) * HG] for g in range(len(DIL_GROUPS))]
    vs = [v[:, :, g * HG:(g + 1) * HG] for g in range(len(DIL_GROUPS))]
    dists, biases = [], []
    for g, (w, d) in enumerate(DIL_GROUPS):
        dist = d * jnp.arange(w // d + 1, dtype=jnp.int32)
        dists.append(dist)
        tbl = rel_bias[:, g * HG:(g + 1) * HG].astype(jnp.float32)
        biases.append(tbl[_t5_bucket(dist)].T)

    def block(t0):
        t = t0 + jnp.arange(Q_BLOCK, dtype=jnp.int32)
        outs, lses = [], []
        for g in range(len(DIL_GROUPS)):
            qb = lax.dynamic_slice_in_dim(qs[g], t0, Q_BLOCK, axis=1)
            idx = t[:, None] - dists[g][None, :]
            valid = idx >= 0
            idx = jnp.maximum(idx, 0)
            kg = ks[g][:, idx]
            vg = vs[g][:, idx]
            logits = jnp.einsum('bqhd,bqkhd->bhqk', qb, kg).astype(jnp.float32)
            logits = logits + biases[g][None, :, None, :]
            logits = jnp.where(valid[None, None], logits, -jnp.inf)
            lse = jax.nn.logsumexp(logits, axis=-1)
            p = jnp.exp(logits - lse[..., None])
            outs.append(jnp.einsum('bhqk,bqkhd->bqhd', p.astype(vg.dtype), vg).astype(jnp.float32))
            lses.append(lse)
        wts = jax.nn.softmax(jnp.stack(lses, axis=0), axis=0)
        wts = wts.transpose(0, 1, 3, 2)[..., None]
        o = jnp.sum(wts * jnp.stack(outs, axis=0), axis=0)
        return o.astype(q.dtype).reshape(B, Q_BLOCK, HG * Dh)

    starts = jnp.arange(S // Q_BLOCK, dtype=jnp.int32) * Q_BLOCK
    o = lax.map(block, starts)
    return o.transpose(1, 0, 2, 3).reshape(B, S, HG * Dh)

def _memory_attention(q, mk, mv):
    B, S, H, Dh = q.shape
    logits = jnp.einsum('bshd,bmhd->bhsm', q, mk).astype(jnp.float32)
    p = jax.nn.softmax(logits, axis=-1)
    o = jnp.einsum('bhsm,bmhd->bshd', p.astype(mv.dtype), mv)
    return o.reshape(B, S, H * Dh)

def setup_inputs(seed: int = 0) -> dict:
    key = jax.random.key(seed)
    ks = jax.random.split(key, 24)
    f32 = jnp.float32

    def w(k, shape, fan_in, mult=1.0):
        return jax.random.normal(k, shape, f32) * (mult * fan_in ** -0.5)

    def gain(k, shape):
        return 1.0 + 0.05 * jax.random.normal(k, shape, f32)

    return {
        "x": jax.random.normal(ks[0], (BATCH, SEQ, D_MODEL), f32),
        "mem": jax.random.normal(ks[1], (BATCH, N_MEM, D_MODEL), f32),
        "rel_bias": 0.2 * jax.random.normal(ks[2], (N_BUCKETS, N_DIL_HEADS), f32),
        "ffn1_norm": gain(ks[3], (DEPTH, D_MODEL)),
        "ffn1_w_gu": w(ks[4], (DEPTH, D_MODEL, 2 * D_FF), D_MODEL),
        "ffn1_w_down": w(ks[5], (DEPTH, D_FF, D_MODEL), D_FF),
        "mix_norm": gain(ks[6], (DEPTH, D_MODEL)),
        "mem_norm": gain(ks[7], (DEPTH, D_MODEL)),
        "w_in": w(ks[8], (DEPTH, D_MODEL, IN_COLS), D_MODEL),
        "w_mem_kv": w(ks[9], (DEPTH, D_MODEL, 2 * X_W), D_MODEL),
        "dil_q_gain": gain(ks[10], (DEPTH, HEAD_DIM)),
        "dil_k_gain": gain(ks[11], (DEPTH, HEAD_DIM)),
        "x_q_gain": gain(ks[12], (DEPTH, HEAD_DIM)),
        "x_k_gain": gain(ks[13], (DEPTH, HEAD_DIM)),
        "w_br_sb": w(ks[14], (DEPTH, SB_W, D_MODEL), SB_W),
        "w_br_dil": w(ks[15], (DEPTH, DIL_OUT_W, D_MODEL), DIL_OUT_W),
        "w_br_x": w(ks[16], (DEPTH, X_W, D_MODEL), X_W),
        "w_out": w(ks[17], (DEPTH, D_MODEL, D_MODEL), D_MODEL),
        "ffn2_norm": gain(ks[18], (DEPTH, D_MODEL)),
        "ffn2_w_gu": w(ks[19], (DEPTH, D_MODEL, 2 * D_FF), D_MODEL),
        "ffn2_w_down": w(ks[20], (DEPTH, D_FF, D_MODEL), D_FF),
    }

def reference(x, mem, rel_bias, ffn1_norm, ffn1_w_gu, ffn1_w_down, mix_norm, mem_norm, w_in,
              w_mem_kv, dil_q_gain, dil_k_gain, x_q_gain, x_k_gain, w_br_sb, w_br_dil, w_br_x,
              w_out, ffn2_norm, ffn2_w_gu, ffn2_w_down):
    B, S, D = x.shape
    M = mem.shape[1]
    scale = 1.0 / math.sqrt(HEAD_DIM)
    split_at = [int(i) for i in np.cumsum([SB_W, SB_W, SB_W, DIL_W, DIL_W, DIL_W, X_W])]
    for l in range(DEPTH):
        x = x + 0.5 * _swiglu(_rmsnorm(x, ffn1_norm[l]), ffn1_w_gu[l], ffn1_w_down[l])

        h = _rmsnorm(x, mix_norm[l])
        proj = h @ w_in[l]
        q_sb, k_sb, v_sb, q_d, k_d, v_d, q_x, gates = jnp.split(proj, split_at, axis=-1)

        o_sb = _stick_breaking(q_sb.reshape(B, S, N_SB_HEADS, HEAD_DIM),
                               k_sb.reshape(B, S, N_SB_HEADS, HEAD_DIM),
                               v_sb.reshape(B, S, N_SB_HEADS, HEAD_DIM))

        qd = _rmsnorm(q_d.reshape(B, S, N_DIL_HEADS, HEAD_DIM), dil_q_gain[l]) * scale
        kd = _rmsnorm(k_d.reshape(B, S, N_DIL_HEADS, HEAD_DIM), dil_k_gain[l])
        o_dil = _dilated_attention(qd, kd, v_d.reshape(B, S, N_DIL_HEADS, HEAD_DIM), rel_bias)

        mn = _rmsnorm(mem, mem_norm[l])
        mk, mv = jnp.split(mn @ w_mem_kv[l], 2, axis=-1)
        mk = _rmsnorm(mk.reshape(B, M, N_X_HEADS, HEAD_DIM), x_k_gain[l])
        mv = mv.reshape(B, M, N_X_HEADS, HEAD_DIM)
        qx = _rmsnorm(q_x.reshape(B, S, N_X_HEADS, HEAD_DIM), x_q_gain[l]) * scale
        o_x = _memory_attention(qx, mk, mv)

        g = jax.nn.sigmoid(gates.astype(jnp.float32)).reshape(B, S, N_BRANCH, D).astype(x.dtype)
        merged = (g[:, :, 0] * (o_sb @ w_br_sb[l])
                  + g[:, :, 1] * (o_dil @ w_br_dil[l])
                  + g[:, :, 2] * (o_x @ w_br_x[l]))
        x = x + merged @ w_out[l]

        x = x + 0.5 * _swiglu(_rmsnorm(x, ffn2_norm[l]), ffn2_w_gu[l], ffn2_w_down[l])
    return x


_drawn_inputs = setup_inputs


def setup_inputs(seed=0):
    import zlib

    import numpy as np

    out = dict(_drawn_inputs(seed))
    spreads = {}
    factors = {'rel_bias': 26.037,
     'ffn1_norm': 2.728,
     'mem_norm': 8.0,
     'dil_q_gain': 8.0,
     'dil_k_gain': 8.0,
     'x_q_gain': 8.0,
     'x_k_gain': 8.0,
     'ffn2_norm': 3.089}
    for name, (base, spread) in spreads.items():
        noise = np.random.default_rng([zlib.crc32(name.encode()), seed]).standard_normal(out[name].shape)
        drawn = base * np.exp(spread * noise) if base else spread * noise
        out[name] = jnp.asarray(drawn.astype(out[name].dtype))
    for name, factor in factors.items():
        out[name] = (out[name] * factor).astype(out[name].dtype)
    return out
```

```python
from contextlib import ExitStack

import numpy as np
import concourse.bass as bass
from concourse import mybir

P = 128
D = 1024
S = 1024
DT = D // P
FF = 2816
FT = FF // P
MEM = 256
MB = MEM // P
HD = 64
HS, HDL, HX = 6, 6, 4
NG = 3
EPS = 1e-6
NEG = -1e30
GT = 2
NGRP = FT // GT
NRAW, NW = 2, 4
AHEAD = 2
BODY = 6 * GT

U_MEM = 0
U_FFN1 = U_MEM + 4
FFN_UNITS = 3 * FT
U_SB = U_FFN1 + FFN_UNITS
U_DIL = U_SB + 9
U_QX = U_DIL + 9
U_MERGE = U_QX + 2
U_OUT = U_MERGE + 4 * DT
U_FFN2 = U_OUT + DT
UNITS = U_FFN2 + FFN_UNITS
BR = (HS * HD + 2 * HD + HX * HD) // P
BR_OF = ((0, 3), (3, 4), (4, 6))

STRIP = 15 * P
G2_AT, G0_AT, G1_AT = 0, 8 * P, 10 * P
DIL = ((128, 1), (512, 4), (2048, 16))
TOE = 1152

F32 = mybir.dt.float32
F32R = mybir.dt.float32r
ALU = mybir.AluOpType
ACT = mybir.ActivationFunctionType
AX = mybir.AxisListType

PROJ = [("norm", MEM), ("norm", MEM), ("turn", MEM), ("turn", MEM)]
PROJ += [("copy", S), ("copy", S), ("turn", S)] * 3
PROJ += [("norm", S)] * 6 + [("turn", S)] * 3 + [("norm", S)] * 2
PR_SB, PR_DIL, PR_QX = 4, 13, 22


def count_before(kinds, n):
    return sum(k in kinds for k, _ in PROJ[:n])


def bank_pieces(lo, hi):
    return [(a, b) for a, b in ((lo, min(hi, 512)), (max(lo, 512), hi)) if a < b]


def layer(nc, x, mem, weights, gains, head_gains, rel_bias, consts, onehot, out):
    ctx = ExitStack()
    with ctx:
        base = -(-nc.sbuf_base // 64) * 64

        def at(name, off, shape, dt=F32):
            return nc.alloc_sbuf_tensor_at(name, shape, dt, offset=base + off)

        def sem(name):
            return ctx.enter_context(nc.semaphore(name))

        K = 1024
        XT = 0
        HH, HL = 32 * K, 64 * K
        RAW = 96 * K
        WH, WL = RAW + 4 * K * NRAW, RAW + 4 * K * (NRAW + NW)
        MISC = WL + 4 * K * NW
        AR = MISC + 10 * K

        xT = at("xT", XT, [P, DT, S])
        h_hi = at("h_hi", HH, [P, DT, S], F32R)
        h_lo = at("h_lo", HL, [P, DT, S], F32R)
        raw = at("raw", RAW, [P, NRAW, 1024])
        w_hi = at("w_hi", WH, [P, NW, 8, P], F32R)
        w_lo = at("w_lo", WL, [P, NW, 8, P], F32R)
        cst = at("cst", MISC, [P, 7, P])
        ident, neg_tri, neg_ones, ones, head_ones, causal, neg_mask = (cst[:, i, :] for i in range(7))
        mkT = at("mkT", MISC + 3584, [P, 2, MEM])
        mv = at("mv", MISC + 3584 + 2048, [P, MB, MEM])
        sm = MISC + 3584 + 4096
        g_raw = at("g_raw", sm, [P, 4, DT])
        g32 = at("g32", sm + 128, [P, 4, DT])
        hg_raw = at("hg_raw", sm + 256, [P, 4])
        hg = at("hg", sm + 288, [P, 4])
        eps_d = at("eps_d", sm + 320, [P, 1])
        eps_h = at("eps_h", sm + 352, [P, 1])
        m_ss = at("m_ss", sm + 384, [P, MB])
        m_rs = at("m_rs", sm + 416, [P, MB])
        b_max = at("b_max", sm + 448, [P, 1])
        b_nmax = at("b_nmax", sm + 480, [P, 1])
        b_den = at("b_den", sm + 512, [P, 1])
        b_rden = at("b_rden", sm + 544, [P, 1])
        x_max = at("x_max", sm + 576, [P, 4])
        x_den = at("x_den", sm + 608, [P, 4])
        x_rden = at("x_rden", sm + 640, [P, 4])

        x_nat = at("x_nat", HH, [P, 8, D])
        m_nat = at("m_nat", HL, [P, MB, D])
        m_sq = at("m_sq", HL + 8 * K, [P, D])
        mT = at("mT", HL + 12 * K, [P, DT, MEM])
        oh = at("oh", AR + 32 * K, [33, NG * TOE])
        mT_hi = at("mT_hi", AR, [P, DT, MEM], F32R)
        mT_lo = at("mT_lo", AR + 8 * K, [P, DT, MEM], F32R)
        rel = at("rel", AR + 16 * K, [33, 6])
        toe = at("toe", AR + 17 * K, [2, NG * TOE])

        a_hi = at("a_hi", AR, [P, 2 * GT, S], F32R)
        a_lo = at("a_lo", AR + 16 * K, [P, 2 * GT, S], F32R)
        silu = at("silu", AR + 32 * K, [P, 2, S])
        glu = at("glu", AR + 40 * K, [P, 2, S])
        norm_bufs = [(at(f"sq{v}", sq_at, [P, 2, S]), at(f"acc{v}", sq_at + 8 * K, [P, S]),
                      at(f"rB{v}", sq_at + 12 * K, [P, S]), at(f"hf{v}", sq_at + 16 * K, [P, 2, S]))
                     for v, sq_at in enumerate((AR + 32 * K, AR))]

        pr_sq = at("pr_sq", AR + 48 * K, [P, S])
        pr_rs = at("pr_rs", AR + 52 * K, [P, S])
        pr_vT = at("pr_vT", AR + 56 * K, [P, S])

        o_sb = at("o_sb", AR, [P, 3, S])
        o_dil = at("o_dil", AR + 12 * K, [P, S])
        o_x = at("o_x", AR + 16 * K, [P, 2, S])
        sb_q = at("sb_q", AR + 24 * K, [P, S])
        sb_k = at("sb_k", AR + 28 * K, [P, S])
        sb_v = at("sb_v", AR + 32 * K, [P, 8, P])
        sb_l = at("sb_l", XT, [P, 2, S])
        sb_sp = at("sb_sp", XT + 8 * K, [P, 2, S])
        sb_sum = at("sb_sum", XT + 16 * K, [P, 2, S])
        sb_a = at("sb_a", XT + 24 * K, [P, 2, S])
        d_qk = at("d_qk", XT, [P, 6, S])
        d_v = at("d_v", XT + 24 * K, [P, 2, 8, P])
        d_v2 = at("d_v2", AR + 16 * K, [P, 8, P])
        bias = at("bias", AR + 20 * K, [P, 2, STRIP])
        d_p = at("d_p", AR + 35 * K, [P, 2, STRIP])
        d_pT = at("d_pT", AR + 50 * K, [P, 2, 512])
        x_q = at("x_q", XT, [P, 2, S])
        x_p = at("x_p", XT + 8 * K, [P, 4, MEM])
        x_pT = at("x_pT", XT + 12 * K, [P, MB, 512])
        oM_hi = at("oM_hi", XT, [P, BR, S], F32R)
        oM_lo = at("oM_lo", AR + 24 * K, [P, BR, S], F32R)
        gate = at("gate", AR + 48 * K, [P, 3, S])
        merged = at("merged", AR, [P, 6, S])
        merged2 = at("merged2", XT + 24 * K, [P, 2, S])
        x_back = at("x_back", AR + 24 * K, [P, DT, S])
        y_nat = at("y_nat", AR, [P, 2, D])

        ps = ctx.enter_context(nc.psum_tensor("ps", [P, 4, 1024], F32))

        x_keep = nc.dram_tensor("x_keep", (P, DT * S), F32, kind="Internal").ap()
        toe_keep = nc.dram_tensor("toe_keep", (2, P, NG * TOE), F32, kind="Internal").ap()

        x_in = [sem(f"x_in{i}") for i in range(8)]
        mem_in, cst_in, gain_in, hgain_in = sem("mem_in"), sem("cst_in"), sem("gain_in"), sem("hgain_in")
        onehot_in, rel_in = sem("onehot_in"), sem("rel_in")
        consts_ready = sem("consts_ready")
        gains_ready = sem("gains_ready")
        raw_in = [sem(f"raw_in{i}") for i in range(NRAW)]
        hi_done, split_done, unit_done = sem("hi_done"), sem("split_done"), sem("unit_done")
        toe_done, toe_kept, toe_out, bias_in = sem("toe_done"), sem("toe_kept"), sem("toe_out"), sem("bias_in")
        m_ss_done, m_rs_done, m_scaled = sem("m_ss_done"), sem("m_rs_done"), sem("m_scaled")
        m_turned, mT_done, mT_hi_done, mT_split = sem("m_turned"), sem("mT_done"), sem("mT_hi_done"), sem("mT_split")
        x_turned, xT_done = sem("x_turned"), sem("xT_done")
        sq_done, acc_done, ss_done = sem("sq_done"), sem("acc_done"), sem("ss_done")
        ln_done, rstd_done = sem("ln_done"), sem("rstd_done")
        hf_done, h_hi_done, h_ready = sem("hf_done"), sem("h_hi_done"), sem("h_ready")
        silu_done, glu_done, a_hi_done, a_ready = sem("silu_done"), sem("glu_done"), sem("a_hi_done"), sem("a_ready")
        down_done, down_added = sem("down_done"), sem("down_added")
        pr_copied, pr_sq_done = sem("pr_copied"), sem("pr_sq_done")
        pr_aux, pr_ln, pr_rstd, pr_final = sem("pr_aux"), sem("pr_ln"), sem("pr_rstd"), sem("pr_final")
        x_kept, x_back_in = sem("x_kept"), sem("x_back_in")
        sb_z, sb_abs, sb_exp, sb_ln = sem("sb_z"), sem("sb_abs"), sem("sb_exp"), sem("sb_ln")
        sb_soft, sb_sp_ready, sb_sum_ready = sem("sb_soft"), sem("sb_sp_ready"), sem("sb_sum_ready")
        sb_cum, sb_a_ready, sb_av, sb_o = sem("sb_cum"), sem("sb_a_ready"), sem("sb_av"), sem("sb_o")
        d_z, d_biased, d_negmax, d_exp, d_rden, d_prob = (sem(f"d_{n}") for n in ("z", "biased", "negmax", "exp", "rden", "prob"))
        d_turned, d_pT_ready, d_pv, d_o, d_gap = (sem(f"d_{n}") for n in ("turned", "pT_ready", "pv", "o", "gap"))
        xa_z, xa_max, xa_sub, xa_exp, xa_sum, xa_rden, xa_prob = (
            sem(f"xa_{n}") for n in ("z", "max", "sub", "exp", "sum", "rden", "prob"))
        xa_turned, xa_pT, xa_pv, xa_o = (sem(f"xa_{n}") for n in ("turned", "pT", "pv", "o"))
        o_hi_done, o_split = sem("o_hi_done"), sem("o_split")
        gate_done, gated, gated_sum = sem("gate_done"), sem("gated"), sem("gated_sum")
        br_done = sem("br_done")
        mg_hi_done, mg_split = sem("mg_hi_done"), sem("mg_split")
        x_added = sem("x_added")
        y_turned, y_ready, y_out = sem("y_turned"), [sem("y_ready0"), sem("y_ready1")], [sem("y_out0"), sem("y_out1")]

        def after(eng, s, value):
            if not isinstance(value, int) or value > 0:
                eng.wait_ge(s, value)

        def at_turn(k, i, step=BODY):
            return k if i is None else step * i + k

        def o_tile(i):
            return o_sb[:, i, :] if i < 3 else o_dil[:, :] if i == 3 else o_x[:, i - 4, :]

        def merged_tile(m):
            return merged[:, m, :] if m < 6 else merged2[:, m - 6, :]

        def v_dil(g):
            return d_v[:, g] if g < 2 else d_v2

        def proj_dest(n):
            if n < 2:
                return mkT[:, n, :]
            if n < 4:
                return mv[:, :, (n - 2) * P:(n - 1) * P]
            if n < PR_DIL:
                return (sb_q[:, :], sb_k[:, :], sb_v[:, :, :])[(n - 4) % 3]
            if n < PR_DIL + 6:
                return d_qk[:, n - PR_DIL, :]
            if n < PR_QX:
                return v_dil(n - PR_DIL - 6)[:, :, :]
            return x_q[:, n - PR_QX, :]

        def proj_gain(n):
            return 3 if n < 2 else 0 if n < PR_DIL + 3 else 1 if n < PR_QX else 2

        def sum_count(s):
            head, i = divmod(s, 8)
            return head * 13 + (1 + 2 * i if i < 7 else 13)

        def ps_flat(lo, hi):
            return ps[:, 0:2, :].rearrange("p a b -> p (a b)")[:, lo:hi]

        def d_chunks(n):
            return sum(-(-len(dilated_plan(i % 8)[1]) // 4) for i in range(n))

        block = ctx.enter_context(nc.Block())

        @block.sync
        def _(sp):
            sp.dma_start(m_nat[:], mem.rearrange("(b p) d -> p b d", p=P)).then_inc(mem_in, 16)
            sp.dma_start(cst[:], consts).then_inc(cst_in, 16)
            sp.dma_start(oh[:], onehot).then_inc(onehot_in, 16)
            sp.dma_start(rel[0:32, :], rel_bias).then_inc(rel_in, 16)
            sp.dma_start(hg_raw[:], head_gains).then_inc(hgain_in, 16)
            sp.dma_start(g_raw[:], gains).then_inc(gain_in, 16)
            for b in range(8):
                sp.dma_start(x_nat[:, b, :], x[b * P:(b + 1) * P, :]).then_inc(x_in[b], 16)

            for r in range(NRAW):
                sp.dma_start(raw[:, r, :], weights[r]).then_inc(raw_in[r], 16)
            with sp.Fori(1, UNITS // NRAW) as i:
                for r in range(NRAW):
                    sp.wait_ge(split_done, NRAW * i + r - NRAW + 1)
                    sp.dma_start(raw[:, r, :], weights[bass.ds(NRAW * i + r, 1)].rearrange("a p n -> p (a n)")
                                 ).then_inc(raw_in[r], 16)
            for b in range(8):
                sp.wait_ge(y_ready[b % 2], b // 2 + 1)
                sp.dma_start(out[b * P:(b + 1) * P, :], y_nat[:, b % 2, :]).then_inc(y_out[b % 2], 16)
            sp.wait_ge(y_out[0], 64)
            sp.wait_ge(y_out[1], 64)

        @block.gpsimd
        def _(pool):
            for s in range(48):
                j = 7 - s % 8
                pool.wait_ge(sb_sp_ready, s + 1)
                if j == 0:
                    continue
                if s:
                    pool.wait_ge(sb_cum, s)
                    pool.wait_ge(sb_sum_ready, sum_count(s - 1))
                a, b = j * P, (j + 1) * P
                nc.gpsimd.tensor_copy(sb_sum[:, (s + 1) % 2, a:b], sb_sp[:, s % 2, a:b]).then_inc(sb_sum_ready, 1)
                if j < 7:
                    nc.gpsimd.tensor_tensor(sb_sum[:, (s + 1) % 2, b:], sb_sum[:, s % 2, b:], sb_sp[:, s % 2, b:],
                                            ALU.add).then_inc(sb_sum_ready, 1)

        @block.scalar
        def _(act):
            def split_hi(k, i=None):
                if i is None and k >= UNITS:
                    return
                act.wait_ge(raw_in[k % NRAW], 16 * (at_turn(k // NRAW, i, BODY // NRAW) + 1))
                after(act, unit_done, at_turn(k, i) - NW + 1)
                nc.scalar.activation(w_hi[:, k % NW].rearrange("p a b -> p (a b)"), raw[:, k % NRAW, :],
                                     ACT.Copy).then_inc(hi_done, 1)

            def square(r, k):
                sq, acc, rB, hf = norm_bufs[r // 2]
                if k > 2:
                    act.wait_ge(acc_done, 7 * r + k - 2)
                nc.scalar.activation(sq[:, k % 2, :] if k else acc[:], xT[:, k, :], ACT.Square).then_inc(sq_done, 1)

            def norm(r):
                sq, acc, rB, hf = norm_bufs[r // 2]
                act.wait_ge(ss_done, r + 1)
                nc.scalar.activation(rB[:], ps[:, 0, :], ACT.Ln, bias=eps_d[:, 0:1]).then_inc(ln_done, 1)
                act.wait_ge(ln_done, r + 1)
                nc.scalar.activation(rB[:], rB[:], ACT.Exp, scale=-0.5).then_inc(rstd_done, 1)
                for k in range(DT):
                    act.wait_ge(hf_done, 8 * r + k + 1)
                    nc.scalar.activation(h_hi[:, k, :], hf[:, k % 2, :], ACT.Copy).then_inc(h_hi_done, 1)

            def ffn_tile(k, t, i=None):
                split_hi(k + AHEAD, i)
                act.wait_ge(unit_done, at_turn(k, i) + 1)
                after(act, glu_done, at_turn(t, i, 2 * GT) - 1)
                nc.scalar.activation(silu[:, t % 2, :], ps[:, 0, :], ACT.Silu).then_inc(silu_done, 1)
                split_hi(k + 1 + AHEAD, i)

            def ffn(f, u0):
                t0, u1 = FT * f, u0 + 2 * GT
                for q in range(GT):
                    ffn_tile(u0 + 2 * q, t0 + q)
                with act.Fori(0, (NGRP - 1) // 2) as i:
                    for half in range(2):
                        k = u1 + 3 * GT * half
                        for q in range(GT):
                            ffn_tile(k + 2 * q, t0 + GT * (1 + half) + q, i)
                        for q in range(GT):
                            split_hi(k + 2 * GT + q + AHEAD, i)
                for q in range(GT):
                    split_hi(u0 + FFN_UNITS - GT + q + AHEAD)

            def proj(n, u):
                split_hi(u + AHEAD)
                kind, w = PROJ[n]
                if kind == "norm":
                    i = count_before(("norm",), n)
                    act.wait_ge(pr_copied, n + 1)
                    if i:
                        act.wait_ge(pr_aux, count_before(("norm", "turn"), n))
                    nc.scalar.activation(pr_sq[:, 0:w], proj_dest(n), ACT.Square).then_inc(pr_sq_done, 1)

            def proj_aux(n):
                kind, w = PROJ[n]
                if kind == "norm":
                    i, a = count_before(("norm",), n), count_before(("norm", "turn"), n)
                    act.wait_ge(pr_aux, a + 1)
                    after(act, pr_final, a)
                    nc.scalar.activation(pr_rs[:, 0:w], ps[:, 3, 0:w], ACT.Ln, bias=eps_h[:, 0:1]).then_inc(pr_ln, 1)
                    act.wait_ge(pr_ln, i + 1)
                    nc.scalar.activation(pr_rs[:, 0:w], pr_rs[:, 0:w], ACT.Exp, scale=-0.5).then_inc(pr_rstd, 1)

            def projections(n0, n1, u0):
                for n in range(n0, n1):
                    proj(n, u0 + n - n0)
                    if n > n0:
                        proj_aux(n - 1)
                proj_aux(n1 - 1)

            act.preload_act_table_set("natural_log_exp_and_others")
            act.wait_ge(mem_in, 16)
            for b in range(MB):
                if b:
                    act.wait_ge(m_ss_done, b)
                nc.scalar.activation(m_sq[:], m_nat[:, b, :], ACT.Square, accum_out=m_ss[:, b:b + 1]).then_inc(m_ss_done, 1)
            act.wait_ge(m_ss_done, MB)
            act.wait_ge(consts_ready, 2)
            nc.scalar.activation(m_rs[:], m_ss[:], ACT.Ln, bias=eps_d[:, 0:1]).then_inc(m_rs_done, 1)
            act.wait_ge(m_rs_done, 1)
            nc.scalar.activation(m_rs[:], m_rs[:], ACT.Exp, scale=-0.5).then_inc(m_rs_done, 1)
            act.wait_ge(toe_kept, NG + 1)
            for hh in range(2):
                act.dma_start(toe_keep[hh:hh + 1, :, :], toe[hh:hh + 1, :].unsqueeze(1).to_broadcast([1, P, NG * TOE])
                              ).then_inc(toe_out, 16)
            for k in range(DT):
                act.wait_ge(mT_done, k + 1)
                nc.scalar.activation(mT_hi[:, k, :], mT[:, k, :], ACT.Copy).then_inc(mT_hi_done, 1)
            split_hi(0)
            split_hi(1)
            projections(0, 4, U_MEM)

            act.wait_ge(xT_done, 8)
            for k in range(DT):
                square(0, k)
            norm(0)
            ffn(0, U_FFN1)
            act.preload_act_table_set("natural_log_exp_and_others")
            for k in range(DT):
                act.wait_ge(down_added, DT * (NGRP - 1) + k + 1)
                square(1, k)
            norm(1)
            act.wait_ge(h_ready, 16)
            act.dma_start(x_keep[:, :], xT[:, :, :].rearrange("p k s -> p (k s)")).then_inc(x_kept, 16)

            def sb_explog(s):
                a = (7 - s % 8) * P
                act.wait_ge(sb_z, s + 1)
                after(act, sb_sp_ready, s - 1)
                nc.scalar.activation(sb_l[:, s % 2, a:], ps[:, s % 2, a:], ACT.Abs).then_inc(sb_abs, 1)
                act.wait_ge(sb_abs, s + 1)
                nc.scalar.activation(sb_l[:, s % 2, a:], sb_l[:, s % 2, a:], ACT.Exp, scale=-1.0).then_inc(sb_exp, 1)
                act.wait_ge(sb_exp, s + 1)
                nc.scalar.activation(sb_l[:, s % 2, a:], sb_l[:, s % 2, a:], ACT.Ln, bias=1.0).then_inc(sb_ln, 1)

            def sb_weights(s):
                a = (7 - s % 8) * P
                act.wait_ge(sb_cum, s + 1)
                after(act, sb_av, s - 1)
                nc.scalar.activation(sb_a[:, s % 2, a:], ps[:, s % 2, a:], ACT.Exp).then_inc(sb_a_ready, 1)

            for pair in range(3):
                projections(PR_SB + 3 * pair, PR_SB + 3 * pair + 3, U_SB + 3 * pair)
                for s in range(16 * pair, 16 * pair + 16):
                    sb_explog(s)
                    if s % 16:
                        sb_weights(s - 1)
                sb_weights(16 * pair + 15)

            act.wait_ge(sb_o, 6)
            act.wait_ge(toe_out, 32)
            for hh in range(2):
                for g, c, w, x0 in dilated_windows():
                    src = bass.AP(toe_keep.tensor, (hh * P * NG + g) * TOE + x0, [[NG * TOE - 1, P], [1, w]])
                    act.dma_start(bias[:, hh, c:c + w], src).then_inc(bias_in, 16)
            projections(PR_DIL, PR_QX, U_DIL)
            chunks = 0
            for n in range(16):
                b = n % 8
                segs, blocks = dilated_plan(b)
                lo, hi = segs[0][0], segs[-1][1]
                act.wait_ge(d_negmax, n + 1)
                if n:
                    act.wait_ge(d_rden, n)
                nc.scalar.activation(d_p[:, n % 2, lo:hi], d_p[:, n % 2, lo:hi], ACT.Exp, bias=b_nmax[:, 0:1],
                                     accum_out=b_den[:, 0:1]).then_inc(d_exp, 1)
                for c in range(-(-len(blocks) // 4)):
                    w = min(4, len(blocks) - 4 * c) * P
                    act.wait_ge(d_turned, chunks + 1)
                    after(act, d_pv, chunks - 1)
                    nc.scalar.activation(d_pT[:, chunks % 2, 0:w], ps[:, 2, (chunks % 2) * 512:(chunks % 2) * 512 + w],
                                         ACT.Copy).then_inc(d_pT_ready, 1)
                    chunks += 1

            projections(PR_QX, PR_QX + 2, U_QX)
            for n in range(8):
                act.wait_ge(xa_sub, n + 1)
                nc.scalar.activation(x_p[:], x_p[:], ACT.Exp).then_inc(xa_exp, 1)
                for b in range(MB):
                    act.wait_ge(xa_turned, 2 * n + b + 1)
                    if n:
                        act.wait_ge(xa_pv, n)
                    nc.scalar.activation(x_pT[:, b, :], ps[:, 1, 512 * b:512 * b + 512], ACT.Copy).then_inc(xa_pT, 1)

            act.wait_ge(xa_o, 8)
            for i in range(BR):
                nc.scalar.activation(oM_hi[:, i, :], o_tile(i), ACT.Copy).then_inc(o_hi_done, 1)
            for m in range(DT):
                u = U_MERGE + 4 * m
                for b in range(3):
                    split_hi(u + b + AHEAD)
                    act.wait_ge(unit_done, u + b + 1)
                    if b:
                        after(act, gated_sum, 2 * (m - 1) + b)
                    else:
                        after(act, gated, 3 * (m - 1) + 1)
                    nc.scalar.activation(gate[:, b, :], ps[:, b, :], ACT.Sigmoid).then_inc(gate_done, 1)
                split_hi(u + 3 + AHEAD)

            act.wait_ge(gated_sum, 16)
            act.dma_start(x_back[:, :, :].rearrange("p k s -> p (k s)"), x_keep[:, :]).then_inc(x_back_in, 16)
            for m in range(DT):
                nc.scalar.activation(h_hi[:, m, :], merged_tile(m), ACT.Copy).then_inc(mg_hi_done, 1)
            act.preload_act_table_set("natural_log_exp_and_others")
            for m in range(DT):
                split_hi(U_OUT + m + AHEAD)
                act.wait_ge(x_added, m + 1)
                square(2, m)
            norm(2)
            ffn(1, U_FFN2)

            for b in range(0, 8, 2):
                act.wait_ge(y_turned, b + 1)
                after(act, y_out[0], 16 * (b // 2))
                nc.scalar.activation(y_nat[:, 0, :], ps[:, 0, :], ACT.Copy).then_inc(y_ready[0], 1)

        def d_out(dve, n):
            hh, b = divmod(n, 8)
            dve.wait_ge(d_pv, d_chunks(n + 1))
            nc.vector.tensor_copy(o_dil[hh * HD:hh * HD + HD, b * P:(b + 1) * P],
                                  ps[hh * HD:hh * HD + HD, 3, (n % 2) * 512:(n % 2) * 512 + P]).then_inc(d_o, 1)

        @block.vector
        def _(dve):
            def split_lo(k, i=None):
                if i is None and k >= UNITS:
                    return
                dve.wait_ge(hi_done, at_turn(k, i) + 1)
                nc.vector.tensor_tensor(w_lo[:, k % NW].rearrange("p a b -> p (a b)"), raw[:, k % NRAW, :],
                                        w_hi[:, k % NW].rearrange("p a b -> p (a b)").bitcast(F32),
                                        ALU.subtract).then_inc(split_done, 1)

            def square_sum(r, k):
                sq, acc, rB, hf = norm_bufs[r // 2]
                dve.wait_ge(sq_done, 8 * r + k + 1)
                if k > 1:
                    dve.wait_ge(acc_done, 7 * r + k - 1)
                nc.vector.tensor_tensor(acc[:], acc[:], sq[:, k % 2, :], ALU.add).then_inc(acc_done, 1)

            def norm_rest(r, gain):
                sq, acc, rB, hf = norm_bufs[r // 2]
                dve.wait_ge(rstd_done, r + 1)
                for k in range(DT + 1):
                    if k < DT:
                        if k > 1:
                            dve.wait_ge(h_ready, 8 * r + k - 1)
                        nc.vector.scalar_tensor_tensor(out=hf[:, k % 2, :], in0=xT[:, k, :], scalar=g32[:, gain, k:k + 1],
                                                       in1=rB[:], op0=ALU.mult, op1=ALU.mult).then_inc(hf_done, 1)
                    if k:
                        dve.wait_ge(h_hi_done, 8 * r + k)
                        nc.vector.tensor_tensor(h_lo[:, k - 1, :], hf[:, (k - 1) % 2, :],
                                                h_hi[:, k - 1, :].bitcast(F32), ALU.subtract).then_inc(h_ready, 1)

            def glu_tile(k, t, slot, i=None):
                split_lo(k - 1 + AHEAD, i)
                split_lo(k + AHEAD, i)
                count = at_turn(t, i, 2 * GT)
                dve.wait_ge(unit_done, at_turn(k, i) + 1)
                dve.wait_ge(silu_done, count + 1)
                after(dve, a_ready, count - 1)
                nc.vector.scalar_tensor_tensor(out=glu[:, t % 2, :], in0=silu[:, t % 2, :], scalar=0.5, in1=ps[:, 1, :],
                                               op0=ALU.mult, op1=ALU.mult).then_inc(glu_done, 1)
                dve.wait_ge(glu_done, count + 1)
                nc.vector.tensor_copy(a_hi[:, slot, :], glu[:, t % 2, :]).then_inc(a_hi_done, 1)
                dve.wait_ge(a_hi_done, count + 1)
                nc.vector.tensor_tensor(a_lo[:, slot, :], glu[:, t % 2, :], a_hi[:, slot, :].bitcast(F32),
                                        ALU.subtract).then_inc(a_ready, 1)

            def add_down(g, k, i=None, finish=None):
                for m in range(DT):
                    if m in (2, 4):
                        split_lo(k + m // 2 - 2 + AHEAD, i)
                    if m < DT - 1:
                        dve.wait_ge(down_done, at_turn((DT - 1) * g + m + 1, i, 2 * (DT - 1)))
                    else:
                        dve.wait_ge(unit_done, at_turn(k + 1, i))
                    nc.vector.tensor_tensor(xT[:, m, :], xT[:, m, :], ps[:, 2 + m % 2, :], ALU.add).then_inc(down_added, 1)
                    if finish:
                        finish(m)

            def ffn(f, u0, finish=None):
                t0, g0, u1 = FT * f, NGRP * f, u0 + 2 * GT
                for q in range(GT):
                    glu_tile(u0 + 2 * q + 1, t0 + q, q)
                with dve.Fori(0, (NGRP - 1) // 2) as i:
                    for half in range(2):
                        k = u1 + 3 * GT * half
                        for q in range(GT):
                            glu_tile(k + 2 * q + 1, t0 + GT * (1 + half) + q, GT * (1 - half) + q, i)
                        add_down(g0 + half, k + 3 * GT - 1, i)
                add_down(g0 + NGRP - 1, u0 + FFN_UNITS - 1, None, finish)

            def proj(n, u):
                split_lo(u + AHEAD)
                kind, w = PROJ[n]
                dve.wait_ge(unit_done, u + 1)
                if kind == "turn":
                    after(dve, pr_aux, count_before(("norm", "turn"), n))
                    nc.vector.tensor_copy(pr_vT[:, 0:w], ps[:, n % 2, 0:w]).then_inc(pr_copied, 1)
                elif kind == "copy" and (n - PR_SB) % 3 == 0:
                    nc.vector.tensor_scalar(proj_dest(n), ps[:, n % 2, :], HD ** -0.5, None, ALU.mult).then_inc(pr_copied, 1)
                else:
                    nc.vector.tensor_copy(proj_dest(n), ps[:, n % 2, 0:w]).then_inc(pr_copied, 1)

            def proj_aux(n):
                kind, w = PROJ[n]
                i, a = count_before(("norm",), n), count_before(("norm", "turn"), n)
                if kind == "norm":
                    dve.wait_ge(pr_rstd, i + 1)
                    c = proj_gain(n)
                    nc.vector.scalar_tensor_tensor(out=proj_dest(n), in0=proj_dest(n), scalar=hg[:, c:c + 1],
                                                   in1=pr_rs[:, 0:w], op0=ALU.mult, op1=ALU.mult).then_inc(pr_final, 1)
                elif kind == "turn":
                    dve.wait_ge(pr_aux, a + 1)
                    nc.vector.tensor_copy(proj_dest(n), ps[:, 2, 0:w].rearrange("p (b c) -> p b c", c=P)).then_inc(pr_final, 1)

            def projections(n0, n1, u0):
                for n in range(n0, n1):
                    proj(n, u0 + n - n0)
                    if n > n0:
                        proj_aux(n - 1)
                proj_aux(n1 - 1)

            nc.vector.memset(eps_d[:], D * EPS).then_inc(consts_ready, 1)
            nc.vector.memset(eps_h[:], HD * EPS).then_inc(consts_ready, 1)
            nc.vector.memset(rel[32:33, :], NEG).then_inc(consts_ready, 1)
            dve.wait_ge(gain_in, 16)
            nc.vector.tensor_scalar(g32[:], g_raw[:], float(D) ** 0.5, None, ALU.mult).then_inc(gains_ready, 1)
            dve.wait_ge(hgain_in, 16)
            nc.vector.tensor_scalar(hg[:, 0:1], hg_raw[:, 0:1], 1.0, None, ALU.mult).then_inc(gains_ready, 1)
            nc.vector.tensor_scalar(hg[:, 1:2], hg_raw[:, 1:2], 8.0, None, ALU.mult).then_inc(gains_ready, 1)
            nc.vector.tensor_scalar(hg[:, 2:3], hg_raw[:, 2:3], 1.0, None, ALU.mult).then_inc(gains_ready, 1)
            nc.vector.tensor_scalar(hg[:, 3:4], hg_raw[:, 3:4], 8.0, None, ALU.mult).then_inc(gains_ready, 1)
            dve.wait_ge(gains_ready, 5)
            dve.wait_ge(m_rs_done, 2)
            for b in range(MB):
                nc.vector.tensor_scalar(m_nat[:, b, :], m_nat[:, b, :], m_rs[:, b:b + 1], None, ALU.mult).then_inc(m_scaled, 1)
            for q in range(NG):
                dve.wait_ge(toe_done, q + 1)
                nc.vector.tensor_copy(toe[:, q * TOE:q * TOE + 1024], ps[0:2, q, :]).then_inc(toe_kept, 1)
            nc.vector.tensor_copy(toe[:, :].rearrange("p (g n) -> p g n", g=NG)[:, :, 1024:TOE],
                                  ps[0:2, 3, 0:NG * P].rearrange("p (g n) -> p g n", g=NG)).then_inc(toe_kept, 1)
            for k in range(DT):
                dve.wait_ge(m_turned, k // 4 + 1)
                nc.vector.tensor_scalar(mT[:, k, :], ps[:, k // 4, (k % 4) * MEM:(k % 4 + 1) * MEM],
                                        g32[:, 3, k:k + 1], None, ALU.mult).then_inc(mT_done, 1)
            for k in range(DT):
                dve.wait_ge(mT_hi_done, k + 1)
                nc.vector.tensor_tensor(mT_lo[:, k, :], mT[:, k, :], mT_hi[:, k, :].bitcast(F32),
                                        ALU.subtract).then_inc(mT_split, 1)
            split_lo(0)
            split_lo(1)
            projections(0, 4, U_MEM)
            for b in range(8):
                dve.wait_ge(x_turned, b + 1)
                nc.vector.tensor_copy(xT[:, :, b * P:(b + 1) * P], ps[:, b % 2, :].rearrange("p (k s) -> p k s", s=P)
                                      ).then_inc(xT_done, 1)
            for k in range(1, DT):
                square_sum(0, k)
            norm_rest(0, 0)
            dve.wait_ge(toe_out, 32)
            ffn(0, U_FFN1, lambda m: square_sum(1, m - 1) if m > 1 else None)
            square_sum(1, DT - 1)
            norm_rest(1, 1)

            def sb_softplus(s):
                a = (7 - s % 8) * P
                dve.wait_ge(sb_ln, s + 1)
                if s >= 2:
                    dve.wait_ge(sb_cum, s - 1)
                    dve.wait_ge(sb_sum_ready, sum_count(s - 2))
                nc.vector.scalar_tensor_tensor(out=sb_sp[:, s % 2, a:], in0=ps[:, s % 2, a:], scalar=0.0,
                                               in1=sb_l[:, s % 2, a:], op0=ALU.max, op1=ALU.add).then_inc(sb_soft, 1)
                dve.wait_ge(sb_soft, s + 1)
                nc.vector.tensor_tensor(sb_sp[:, s % 2, a:a + P], sb_sp[:, s % 2, a:a + P], causal,
                                        ALU.mult).then_inc(sb_sp_ready, 1)

            def sb_out(head):
                r = (head % 2) * HD
                dve.wait_ge(sb_av, 8 * head + 8)
                nc.vector.tensor_copy(o_sb[r:r + HD, head // 2, :], ps[r:r + HD, 2, :]).then_inc(sb_o, 1)

            for pair in range(3):
                if pair == 0:
                    dve.wait_ge(x_kept, 16)
                projections(PR_SB + 3 * pair, PR_SB + 3 * pair + 3, U_SB + 3 * pair)
                s0 = 16 * pair
                for s in range(s0, s0 + 16):
                    sb_softplus(s)
                    if s == s0 + 8:
                        sb_out(2 * pair)
                sb_out(2 * pair + 1)

            projections(PR_DIL, PR_QX, U_DIL)
            dve.wait_ge(bias_in, 16 * 2 * 7)
            gap_done = 0
            for n in range(16):
                hh, b = divmod(n, 8)
                segs, blocks = dilated_plan(b)
                lo, hi = segs[0][0], segs[-1][1]
                dve.wait_ge(d_z, n + 1)
                if n > 1:
                    dve.wait_ge(d_turned, d_chunks(n - 1))
                if n:
                    dve.wait_ge(d_exp, n)
                if len(segs) == 1:
                    nc.vector.tensor_tensor_reduce(d_p[:, n % 2, lo:hi], ps_flat(lo, hi), bias[:, hh, lo:hi], 1.0, -3e38,
                                                   ALU.add, ALU.max, b_max[:, 0:1]).then_inc(d_biased, 1)
                else:
                    for c, d in segs:
                        nc.vector.tensor_tensor(d_p[:, n % 2, c:d], ps_flat(c, d), bias[:, hh, c:d], ALU.add).then_inc(d_gap, 1)
                    nc.vector.memset(d_p[:, n % 2, segs[0][1]:segs[1][0]], NEG).then_inc(d_gap, 1)
                    gap_done += 3
                    dve.wait_ge(d_gap, gap_done)
                    nc.vector.tensor_reduce(b_max[:, 0:1], d_p[:, n % 2, lo:hi], AX.X, ALU.max).then_inc(d_biased, 1)
                dve.wait_ge(d_biased, n + 1)
                nc.vector.tensor_scalar(b_nmax[:], b_max[:], -1.0, None, ALU.mult).then_inc(d_negmax, 1)
                dve.wait_ge(d_exp, n + 1)
                after(dve, d_prob, n)
                nc.vector.reciprocal(b_rden[:], b_den[:]).then_inc(d_rden, 1)
                dve.wait_ge(d_rden, n + 1)
                nc.vector.tensor_scalar(d_p[:, n % 2, lo:hi], d_p[:, n % 2, lo:hi], b_rden[:, 0:1], None,
                                        ALU.mult).then_inc(d_prob, 1)
                if n:
                    d_out(dve, n - 1)
            d_out(dve, 15)

            projections(PR_QX, PR_QX + 2, U_QX)
            for n in range(8):
                h, half = divmod(n, 2)
                r = (h % 2) * HD
                z = ps[:, 0, :].rearrange("p (b m) -> p b m", b=4)
                dve.wait_ge(xa_z, n + 1)
                after(dve, xa_prob, n)
                nc.vector.tensor_reduce(x_max[:], z, AX.X, ALU.max).then_inc(xa_max, 1)
                dve.wait_ge(xa_max, n + 1)
                if n:
                    dve.wait_ge(xa_turned, 2 * n)
                nc.vector.tensor_tensor(x_p[:], z, x_max[:].unsqueeze(2).to_broadcast([P, 4, MEM]),
                                        ALU.subtract).then_inc(xa_sub, 1)
                dve.wait_ge(xa_exp, n + 1)
                nc.vector.tensor_reduce(x_den[:], x_p[:], AX.X, ALU.add).then_inc(xa_sum, 1)
                dve.wait_ge(xa_sum, n + 1)
                nc.vector.reciprocal(x_rden[:], x_den[:]).then_inc(xa_rden, 1)
                dve.wait_ge(xa_rden, n + 1)
                nc.vector.tensor_tensor(x_p[:], x_p[:], x_rden[:].unsqueeze(2).to_broadcast([P, 4, MEM]),
                                        ALU.mult).then_inc(xa_prob, 1)
                dve.wait_ge(xa_pv, n + 1)
                nc.vector.tensor_copy(o_x[r:r + HD, h // 2, 512 * half:512 * half + 512],
                                      ps[r:r + HD, 2, 0:512]).then_inc(xa_o, 1)

            for i in range(BR):
                dve.wait_ge(o_hi_done, i + 1)
                nc.vector.tensor_tensor(oM_lo[:, i, :], o_tile(i), oM_hi[:, i, :].bitcast(F32),
                                        ALU.subtract).then_inc(o_split, 1)
            for m in range(DT):
                u = U_MERGE + 4 * m
                for q in range(4):
                    split_lo(u + q + AHEAD)
                for b in range(3):
                    pair = (3, 0, 1)[b]
                    dve.wait_ge(gate_done, 3 * m + b + 1)
                    if b < 2:
                        dve.wait_ge(br_done, 2 * m + b + 1)
                    else:
                        dve.wait_ge(unit_done, u + 4)
                    to = merged_tile(m) if b == 0 else gate[:, b, :]
                    nc.vector.tensor_tensor(to, gate[:, b, :], ps[:, pair, :], ALU.mult).then_inc(gated, 1)
                for b in range(1, 3):
                    dve.wait_ge(gated, 3 * m + 3)
                    if b == 2:
                        dve.wait_ge(gated_sum, 2 * m + 1)
                    nc.vector.tensor_tensor(merged_tile(m), merged_tile(m), gate[:, b, :], ALU.add).then_inc(gated_sum, 1)

            for m in range(DT):
                dve.wait_ge(mg_hi_done, m + 1)
                nc.vector.tensor_tensor(h_lo[:, m, :], merged_tile(m), h_hi[:, m, :].bitcast(F32),
                                        ALU.subtract).then_inc(mg_split, 1)
            dve.wait_ge(x_back_in, 16)
            dve.wait_ge(mg_split, DT)
            for m in range(DT):
                split_lo(U_OUT + m + AHEAD)
                dve.wait_ge(unit_done, U_OUT + m + 1)
                nc.vector.tensor_tensor(xT[:, m, :], x_back[:, m, :], ps[:, 2 + m % 2, :], ALU.add).then_inc(x_added, 1)
                if m > 1:
                    square_sum(2, m - 1)
            square_sum(2, DT - 1)
            norm_rest(2, 2)
            ffn(1, U_FFN2)

            for b in range(1, 8, 2):
                dve.wait_ge(y_turned, b + 1)
                after(dve, y_out[1], 16 * (b // 2))
                nc.vector.tensor_copy(y_nat[:, 1, :], ps[:, 1, :]).then_inc(y_ready[1], 1)

        @block.tensor
        def _(pe):
            def mm(o, a, b, start, stop):
                return pe.matmul(o, a, b, start=start, stop=stop, skip_group_check=True)

            def product(pair, slot, hi, lo, width, tiles=DT, w0=0, there=None):
                halves = [(c, min(c + 512, width)) for c in range(0, width, 512)]
                for k in range(tiles):
                    if there:
                        there(k)
                    first, final = k == 0, k == tiles - 1
                    for c, d in halves:
                        mm(ps[:, pair, c:d], w_hi[:, slot, w0 + k, :], hi(k)[:, c:d], first, False)
                        mm(ps[:, pair, c:d], w_hi[:, slot, w0 + k, :], lo(k)[:, c:d], False, False)
                    for c, d in halves:
                        last = mm(ps[:, pair, c:d], w_lo[:, slot, w0 + k, :], hi(k)[:, c:d], False, final)
                return last

            def hh(k):
                return h_hi[:, k, :]

            def hl(k):
                return h_lo[:, k, :]

            def gate_up(k, t, i=None, there=None):
                for part in range(2):
                    pe.wait_ge(split_done, at_turn(k, i) + part + 1)
                    after(pe, (silu_done, glu_done)[part], at_turn(t, i, 2 * GT))
                    product(part, (k + part) % NW, hh, hl, S, there=there if part == 0 else None).then_inc(unit_done, 1)

            def down(g, k, slot, i=None):
                pe.wait_ge(split_done, at_turn(k, i) + GT)
                pe.wait_ge(a_ready, at_turn(GT * g, i, 2 * GT) + GT)
                for m in range(DT):
                    pair = 2 + m % 2
                    if m >= 2 or i is None:
                        pe.wait_ge(down_added, at_turn(DT * g, i, 2 * DT) + m - 1)
                    for q in range(GT):
                        s = (k + q) % NW
                        for c in (0, 512):
                            mm(ps[:, pair, c:c + 512], w_hi[:, s, m, :], a_hi[:, slot + q, c:c + 512], q == 0, False)
                            mm(ps[:, pair, c:c + 512], w_hi[:, s, m, :], a_lo[:, slot + q, c:c + 512], False, False)
                        for c in (0, 512):
                            last = mm(ps[:, pair, c:c + 512], w_lo[:, s, m, :], a_hi[:, slot + q, c:c + 512], False, q == GT - 1)
                    if m < DT - 1:
                        last.then_inc(down_done, 1)
                    else:
                        last.then_inc(unit_done, GT)

            def ffn(f, u0, r):
                t0, g0, u1 = FT * f, NGRP * f, u0 + 2 * GT
                gate_up(u0, t0, there=lambda k: pe.wait_ge(h_ready, 8 * r + k + 1))
                for q in range(1, GT):
                    gate_up(u0 + 2 * q, t0 + q)
                with pe.Fori(0, (NGRP - 1) // 2) as i:
                    for half in range(2):
                        k = u1 + 3 * GT * half
                        for q in range(GT):
                            gate_up(k + 2 * q, t0 + GT * (1 + half) + q, i)
                        down(g0 + half, k + 2 * GT, GT * half, i)
                down(g0 + NGRP - 1, u0 + FFN_UNITS - GT, 0)

            def norm_sum(r):
                acc = norm_bufs[r // 2][1]
                pe.wait_ge(acc_done, 7 * r + 7)
                for c in (0, 512):
                    last = mm(ps[:, 0, c:c + 512], ones, acc[:, c:c + 512], True, True)
                last.then_inc(ss_done, 1)

            def proj(n, u, hi, lo, there=None):
                kind, w = PROJ[n]
                pe.wait_ge(split_done, u + 1)
                if n >= 2:
                    pe.wait_ge(pr_copied, n - 1)
                product(n % 2, u % NW, hi, lo, w, there=there).then_inc(unit_done, 1)

            def proj_aux(n):
                kind, w = PROJ[n]
                i, a = count_before(("norm",), n), count_before(("norm", "turn"), n)
                if kind == "norm":
                    pe.wait_ge(pr_sq_done, i + 1)
                    after(pe, pr_final, a)
                    for c in range(0, w, 512):
                        d = min(w, c + 512)
                        last = mm(ps[:, 3, c:d], head_ones, pr_sq[:, c:d], True, True)
                    last.then_inc(pr_aux, 1)
                elif kind == "turn":
                    pe.wait_ge(pr_copied, n + 1)
                    after(pe, pr_final, a)
                    for b in range(w // P):
                        last = pe.transpose(ps[:, 2, b * P:(b + 1) * P], pr_vT[:, b * P:(b + 1) * P], ident)
                    last.then_inc(pr_aux, 1)

            def projections(n0, n1, u0, hi, lo, there=None):
                for n in range(n0, n1):
                    proj(n, u0 + n - n0, hi, lo, there if n == n0 else None)
                    if n > n0:
                        proj_aux(n - 1)
                proj_aux(n1 - 1)

            pe.wait_ge(onehot_in, 16)
            pe.wait_ge(rel_in, 16)
            pe.wait_ge(consts_ready, 3)
            for g in range(NG):
                for c in (0, 512):
                    mm(ps[0:2, g, c:c + 512], rel[:, 2 * g:2 * g + 2], oh[:, g * TOE + c:g * TOE + c + 512], True, True)
                last = mm(ps[0:2, 3, g * P:(g + 1) * P], rel[:, 2 * g:2 * g + 2],
                          oh[:, g * TOE + 1024:(g + 1) * TOE], True, True)
                last.then_inc(toe_done, 1)
            pe.wait_ge(toe_kept, NG + 1)
            pe.wait_ge(cst_in, 16)
            pe.wait_ge(m_scaled, MB)
            for k in range(DT):
                for b in range(MB):
                    last = pe.transpose(ps[:, k // 4, (k % 4) * MEM + b * P:(k % 4) * MEM + (b + 1) * P],
                                        m_nat[:, b, k * P:(k + 1) * P], ident)
                if k % 4 == 3:
                    last.then_inc(m_turned, 1)
            pe.wait_ge(mT_done, DT)
            projections(0, 4, U_MEM, lambda k: mT_hi[:, k, :], lambda k: mT_lo[:, k, :],
                        there=lambda k: pe.wait_ge(mT_split, k + 1))
            pe.wait_ge(pr_copied, 4)
            pe.wait_ge(pr_final, 4)
            for b in range(8):
                pe.wait_ge(x_in[b], 16)
                if b >= 2:
                    pe.wait_ge(xT_done, b - 1)
                for k in range(DT):
                    last = pe.transpose(ps[:, b % 2, k * P:(k + 1) * P], x_nat[:, b, k * P:(k + 1) * P], ident)
                last.then_inc(x_turned, 1)
            norm_sum(0)
            ffn(0, U_FFN1, 0)
            norm_sum(1)

            def sb_scores(s):
                head, j = s // 8, 7 - s % 8
                r = (head % 2) * HD
                after(pe, sb_a_ready, s - 1)
                for c, d in bank_pieces(j * P, S):
                    last = mm(ps[:, s % 2, c:d], sb_k[r:r + HD, j * P:(j + 1) * P], sb_q[r:r + HD, c:d], True, False)
                last.then_inc(sb_z, 1)

            def sb_cumulate(s):
                j = 7 - s % 8
                pe.wait_ge(sb_sp_ready, s + 1)
                if j < 7:
                    pe.wait_ge(sb_sum_ready, sum_count(s - 1))
                for c, d in bank_pieces(j * P, S):
                    mm(ps[:, s % 2, c:d], neg_tri, sb_sp[:, s % 2, c:d], False, False)
                for c, d in bank_pieces((j + 1) * P, S):
                    mm(ps[:, s % 2, c:d], neg_ones, sb_sum[:, s % 2, c:d], False, False)
                mm(ps[:, s % 2, j * P:(j + 1) * P], ident, neg_mask, False, True).then_inc(sb_cum, 1)

            def sb_values(s):
                head, j = s // 8, 7 - s % 8
                r = (head % 2) * HD
                pe.wait_ge(sb_a_ready, s + 1)
                if j == 7:
                    after(pe, sb_o, head)
                for c, d in bank_pieces(j * P, S):
                    last = mm(ps[r:r + HD, 2, c:d], sb_v[:, j, r:r + HD], sb_a[:, s % 2, c:d], j == 7 or (j == 3 and c < 512), j == 0)
                last.then_inc(sb_av, 1)

            for pair in range(3):
                there = (lambda k: pe.wait_ge(h_ready, 8 + k + 1)) if pair == 0 else None
                after(pe, sb_o, 2 * pair)
                projections(PR_SB + 3 * pair, PR_SB + 3 * pair + 3, U_SB + 3 * pair, hh, hl, there)
                pe.wait_ge(pr_copied, PR_SB + 3 * pair + 3)
                pe.wait_ge(pr_final, count_before(("norm", "turn"), PR_SB + 3 * pair + 3))
                s0 = 16 * pair
                sb_scores(s0)
                for s in range(s0, s0 + 16):
                    if s + 1 < s0 + 16:
                        sb_scores(s + 1)
                    if s > s0:
                        sb_values(s - 1)
                    sb_cumulate(s)
                sb_values(s0 + 15)

            pe.wait_ge(sb_o, 6)
            projections(PR_DIL, PR_QX, U_DIL, hh, hl)
            pe.wait_ge(pr_copied, PR_QX)
            pe.wait_ge(pr_final, count_before(("norm", "turn"), PR_QX))

            def d_scores(n):
                head, b = divmod(n, 8)
                r = head * HD
                after(pe, d_biased, n)
                q = lambda g: d_qk[r:r + HD, g, b * P:(b + 1) * P]
                kk = lambda g, c, d: d_qk[r:r + HD, 3 + g, c:d]
                a = (7 - b) * P
                for c, d in bank_pieces(a, 1024):
                    mm(ps_flat(c, d), q(2), kk(2, c - a, d - a), True, True)
                lo = max(b - 1, 0)
                mm(ps_flat(G0_AT + (lo - b + 1) * P, G0_AT + 2 * P), q(0), kk(0, lo * P, (b + 1) * P), True, True)
                for i in range(min(b, 4) + 1):
                    last = mm(ps_flat(G1_AT + i * P, G1_AT + (i + 1) * P), q(1), kk(1, (b - i) * P, (b - i + 1) * P), True, True)
                last.then_inc(d_z, 1)

            def d_values(n):
                head, b = divmod(n, 8)
                r = head * HD
                blocks = dilated_plan(b)[1]
                chunk0 = d_chunks(n)
                nch = -(-len(blocks) // 4)
                pe.wait_ge(d_prob, n + 1)
                for c in range(nch + 1):
                    if c < nch:
                        ch = chunk0 + c
                        after(pe, d_pT_ready, ch - 1)
                        for i, (at_, _, _) in enumerate(blocks[4 * c:4 * c + 4]):
                            col = (ch % 2) * 512 + i * P
                            last = pe.transpose(ps[:, 2, col:col + P], d_p[:, n % 2, at_:at_ + P], ident)
                        last.then_inc(d_turned, 1)
                    if c:
                        ch = chunk0 + c - 1
                        pe.wait_ge(d_pT_ready, ch + 1)
                        if c == 1:
                            after(pe, d_o, n - 1)
                        for i, (_, g, kb) in enumerate(blocks[4 * c - 4:4 * c]):
                            last = mm(ps[r:r + HD, 3, (n % 2) * 512:(n % 2) * 512 + P], v_dil(g)[:, kb, r:r + HD],
                                      d_pT[:, ch % 2, i * P:(i + 1) * P], c == 1 and i == 0, 4 * c - 4 + i == len(blocks) - 1)
                        last.then_inc(d_pv, 1)

            d_scores(0)
            for n in range(16):
                if n + 1 < 16:
                    d_scores(n + 1)
                d_values(n)

            pe.wait_ge(d_o, 16)
            projections(PR_QX, PR_QX + 2, U_QX, hh, hl)
            pe.wait_ge(pr_copied, PR_QX + 2)
            pe.wait_ge(pr_final, count_before(("norm", "turn"), PR_QX + 2))
            for n in range(8):
                h, half = divmod(n, 2)
                r = (h % 2) * HD
                after(pe, xa_sub, n)
                for b in range(4):
                    q0 = (4 * half + b) * P
                    last = mm(ps[:, 0, b * MEM:(b + 1) * MEM], x_q[r:r + HD, h // 2, q0:q0 + P], mkT[r:r + HD, h // 2, :], True, True)
                last.then_inc(xa_z, 1)
                pe.wait_ge(xa_prob, n + 1)
                after(pe, xa_pT, 2 * n)
                for mb in range(MB):
                    for b in range(4):
                        last = pe.transpose(ps[:, 1, mb * 512 + b * P:mb * 512 + (b + 1) * P], x_p[:, b, mb * P:(mb + 1) * P], ident)
                    last.then_inc(xa_turned, 1)
                after(pe, xa_o, n)
                for mb in range(MB):
                    pe.wait_ge(xa_pT, 2 * n + mb + 1)
                    last = mm(ps[r:r + HD, 2, 0:512], mv[:, mb, h * HD:(h + 1) * HD], x_pT[:, mb, :], mb == 0, mb == MB - 1)
                last.then_inc(xa_pv, 1)

            pe.wait_ge(xa_o, 8)
            for m in range(DT):
                u = U_MERGE + 4 * m
                for b in range(3):
                    pe.wait_ge(split_done, u + b + 1)
                    if m and b < 2:
                        pe.wait_ge(gated, 3 * (m - 1) + b + 2)
                    if m and b == 2:
                        pe.wait_ge(gate_done, 3 * m)
                    product(b, (u + b) % NW, hh, hl, S).then_inc(unit_done, 1)
                pe.wait_ge(split_done, u + 4)
                if m == 0:
                    pe.wait_ge(o_split, BR)
                for b in range(3):
                    if b == 0:
                        after(pe, gated, 3 * (m - 1) + 1)
                    else:
                        pe.wait_ge(gate_done, 3 * m + b)
                    k0, k1 = BR_OF[b]
                    product((3, 0, 1)[b], (u + 3) % NW, lambda k: oM_hi[:, k0 + k, :], lambda k: oM_lo[:, k0 + k, :], S,
                            tiles=k1 - k0, w0=k0).then_inc(br_done if b < 2 else unit_done, 1)

            for m in range(DT):
                u = U_OUT + m
                pe.wait_ge(split_done, u + 1)
                if m >= 2:
                    pe.wait_ge(x_added, m - 1)
                product(2 + m % 2, u % NW, hh, hl, S, there=(lambda k: pe.wait_ge(mg_split, k + 1)) if m == 0 else None
                        ).then_inc(unit_done, 1)
            norm_sum(2)
            ffn(1, U_FFN2, 2)

            pe.wait_ge(down_added, 16 * NGRP)
            for b in range(8):
                after(pe, y_ready[b % 2], b // 2)
                for k in range(DT):
                    last = pe.transpose(ps[:, b % 2, k * P:(k + 1) * P], xT[:, k, b * P:(b + 1) * P], ident)
                last.then_inc(y_turned, 1)


def dilated_plan(b):
    g2 = [((7 - b + k) * P, 2, k) for k in range(b + 1)]
    g0 = [(G0_AT + (k - b + 1) * P, 0, k) for k in range(max(b - 1, 0), b + 1)]
    g1 = [(G1_AT + i * P, 1, b - i) for i in range(min(b, 4) + 1)]
    end = G1_AT + (min(b, 4) + 1) * P
    segs = [((7 - b) * P, end)] if b else [(7 * P, 8 * P), (9 * P, end)]
    return segs, g2 + g0 + g1


def dilated_windows():
    back = TOE - 1 - P
    return ([(2, G2_AT, 8 * P, back - 7 * P), (0, G0_AT, 2 * P, back - P)]
            + [(1, G1_AT + i * P, P, back - i * P) for i in range(5)])


def t5_bucket(dist):
    exact, last, farthest = 16, 31, 2048
    if dist < exact:
        return dist
    f = np.float32
    large = exact + int(f(np.log(f(dist) / f(exact))) / f(np.log(farthest / exact)) * f(exact))
    return min(large, last)


def bias_onehot():
    t = np.zeros((33, NG, TOE), np.float32)
    for g, (w, d) in enumerate(DIL):
        for x in range(TOE):
            dist = S - 1 - x
            ok = 0 <= dist <= w and dist % d == 0
            t[t5_bucket(dist) if ok else 32, g, x] = 1.0
    return t.reshape(33, NG * TOE)


def constants():
    i, j = np.arange(P)[:, None], np.arange(P)[None, :]
    one = np.ones((P, P))
    tiles = [i == j, -1.0 * (i >= j), -one, one, i // HD == j // HD, i < j, NEG * (i >= j)]
    return np.ascontiguousarray(np.stack([np.asarray(t, np.float32) for t in tiles], axis=1))


def column_units(w, tiles):
    n = w.shape[0] // P
    return [w[:, c * P:(c + 1) * P].reshape(n, P, P).transpose(1, 0, 2).reshape(P, n * P) for c in tiles]


def swiglu_units(w_gu, w_down):
    def gu(g):
        return column_units(w_gu, [c for t in range(GT * g, GT * g + GT) for c in (t, FT + t)])

    def down(g):
        return [w_down[f * P:(f + 1) * P] for f in range(GT * g, GT * g + GT)]

    units = gu(0)
    for g in range(1, NGRP):
        units += gu(g) + down(g - 1)
    return units + down(NGRP - 1)


def weight_units(w_mem_kv, f1_gu, f1_down, w_in, w_br, w_out, f2_gu, f2_down):
    units = column_units(w_mem_kv, range(4)) + swiglu_units(f1_gu, f1_down)
    units += column_units(w_in, [q + 3 * i for q in range(3) for i in range(3)])
    units += column_units(w_in, range(9, 20))
    for m in range(DT):
        units += column_units(w_in, [20 + b * DT + m for b in range(3)])
        units += [np.pad(column_units(w_br, [m])[0], ((0, 0), (0, (DT - BR) * P)))]
    units += column_units(w_out, range(DT)) + swiglu_units(f2_gu, f2_down)
    return np.ascontiguousarray(np.stack(units))


_ORDER = ["x", "mem", "weights", "gains", "head_gains", "rel_bias", "consts", "onehot"]


def kernel(**inputs):
    import concourse.bacc as _bacc
    from concourse.bass_utils import run_bass_kernel_spmd as _run

    a = {k: np.asarray(v) for k, v in inputs.items()}
    w_br = np.concatenate([a["w_br_sb"][0], a["w_br_dil"][0], a["w_br_x"][0]], axis=0)
    arrays = {
        "x": a["x"][0],
        "mem": a["mem"][0],
        "weights": weight_units(a["w_mem_kv"][0], a["ffn1_w_gu"][0], a["ffn1_w_down"][0], a["w_in"][0], w_br,
                                a["w_out"][0], a["ffn2_w_gu"][0], a["ffn2_w_down"][0]),
        "gains": np.stack([a[n][0].reshape(DT, P).T for n in ("ffn1_norm", "mix_norm", "ffn2_norm", "mem_norm")], axis=1),
        "head_gains": np.stack([np.tile(a[n][0], 2) for n in ("dil_q_gain", "dil_k_gain", "x_q_gain", "x_k_gain")], axis=1),
        "rel_bias": a["rel_bias"],
        "consts": constants(),
        "onehot": bias_onehot(),
    }
    nc = _bacc.Bacc("TRN2", target_bir_lowering=False, num_devices=1)
    arrays = {f"in_{n}": np.ascontiguousarray(v) for n, v in arrays.items()}
    args = [nc.dram_tensor(f"in_{n}", arrays[f"in_{n}"].shape, F32, kind="ExternalInput").ap() for n in _ORDER]
    out = nc.dram_tensor("out_0", (S, D), F32, kind="ExternalOutput").ap()
    layer(nc, *args, out)
    r = _run(nc, [arrays], core_ids=[0])
    return r.results[0]["out_0"].reshape(1, S, D)
```

```python
from contextlib import ExitStack

import numpy as np
import concourse.bass as bass
from concourse import mybir

P = 128
D = 1024
S = 1024
DT = D // P
FF = 2816
FT = FF // P
MEM = 256
MB = MEM // P
HD = 64
HS, HDL, HX = 6, 6, 4
NG = 3
EPS = 1e-6
NEG = -1e30
GT = 2
NGRP = FT // GT
NRAW, NW = 2, 3
AHEAD = 2
BODY = 6 * GT

U_MEM = 0
U_FFN1 = U_MEM + 4
FFN_UNITS = 3 * FT
U_SB = U_FFN1 + FFN_UNITS
U_QX = U_SB + 9
U_DIL = U_QX + 2
U_MERGE = U_DIL + 9
U_OUT = U_MERGE + 4 * DT
U_FFN2 = U_OUT + DT
UNITS = U_FFN2 + FFN_UNITS
BR = (HS * HD + 2 * HD + HX * HD) // P
BR_OF = ((0, 3), (3, 4), (4, 6))

STRIP = 15 * P
G2_AT, G0_AT, G1_AT = 0, 8 * P, 10 * P
DIL = ((128, 1), (512, 4), (2048, 16))
TOE = 1152

F32 = mybir.dt.float32
F32R = mybir.dt.float32r
ALU = mybir.AluOpType
ACT = mybir.ActivationFunctionType
AX = mybir.AxisListType

PROJ = [("norm", MEM), ("norm", MEM), ("turn", MEM), ("turn", MEM)]
PROJ += [("copy", S), ("copy", S), ("turn", S)] * 3
PROJ += [("norm", S)] * 2 + [("norm", S)] * 6 + [("turn", S)] * 3
PR_SB, PR_QX, PR_DIL = 4, 13, 15
PR_BESIDE = PR_SB + 3


def count_before(kinds, n):
    return sum(k in kinds for k, _ in PROJ[:n])


def aux_before(n):
    return count_before(("norm", "turn"), n)


def proj_unit(n):
    return U_MEM + n if n < PR_SB else U_SB + n - PR_SB


def proj_pair(n):
    return n % 2 if n < PR_BESIDE else 3 if n < PR_DIL else 2 + (n - PR_DIL) % 2


def aux_pair(n):
    return proj_pair(n) if n >= PR_BESIDE else 3 if PROJ[n][0] == "norm" else 2


def beside_sb(pair):
    return range(PR_BESIDE + 3 * pair, min(PR_BESIDE + 3 * pair + 3, PR_DIL))


SB_EVERY = 5


def bank_pieces(lo, hi):
    return [(a, b) for a, b in ((lo, min(hi, 512)), (max(lo, 512), hi)) if a < b]


def layer(nc, x, mem, weights, gains, head_gains, rel_bias, consts, onehot, out):
    ctx = ExitStack()
    with ctx:
        base = -(-nc.sbuf_base // 64) * 64

        def at(name, off, shape, dt=F32):
            return nc.alloc_sbuf_tensor_at(name, shape, dt, offset=base + off)

        def sem(name):
            return ctx.enter_context(nc.semaphore(name))

        K = 1024
        XT = 0
        HH, HL = 32 * K, 64 * K
        RAW = 96 * K
        WH, WL = RAW + 4 * K * NRAW, RAW + 4 * K * (NRAW + NW)
        MISC = WL + 4 * K * NW
        AR = MISC + 10 * K

        xT = at("xT", XT, [P, DT, S])
        h_hi = at("h_hi", HH, [P, DT, S], F32R)
        h_lo = at("h_lo", HL, [P, DT, S], F32R)
        raw = at("raw", RAW, [P, NRAW, 1024])
        w_hi = at("w_hi", WH, [P, NW, 8, P], F32R)
        w_lo = at("w_lo", WL, [P, NW, 8, P], F32R)
        cst = at("cst", MISC, [P, 7, P])
        ident, neg_tri, neg_ones, ones, head_ones, causal, neg_mask = (cst[:, i, :] for i in range(7))
        mkT = at("mkT", MISC + 3584, [P, 2, MEM])
        mv = at("mv", MISC + 3584 + 2048, [P, MB, MEM])
        sm = MISC + 3584 + 4096
        g_raw = at("g_raw", sm, [P, 4, DT])
        g32 = at("g32", sm + 128, [P, 4, DT])
        hg_raw = at("hg_raw", sm + 256, [P, 4])
        hg = at("hg", sm + 288, [P, 4])
        eps_d = at("eps_d", sm + 320, [P, 1])
        eps_h = at("eps_h", sm + 352, [P, 1])
        m_ss = at("m_ss", sm + 384, [P, MB])
        m_rs = at("m_rs", sm + 416, [P, MB])
        b_max = at("b_max", sm + 448, [P, 1])
        b_nmax = at("b_nmax", sm + 480, [P, 1])
        b_den = at("b_den", sm + 512, [P, 1])
        b_rden = at("b_rden", sm + 544, [P, 1])
        x_max = at("x_max", sm + 576, [P, 4])
        x_den = at("x_den", sm + 608, [P, 4])
        x_rden = at("x_rden", sm + 640, [P, 4])

        x_nat = at("x_nat", HH, [P, 8, D])
        m_nat = at("m_nat", HL, [P, MB, D])
        m_sq = at("m_sq", HL + 8 * K, [P, D])
        mT = at("mT", HL + 12 * K, [P, DT, MEM])
        oh = at("oh", AR + 32 * K, [33, NG * TOE])
        mT_hi = at("mT_hi", AR, [P, DT, MEM], F32R)
        mT_lo = at("mT_lo", AR + 8 * K, [P, DT, MEM], F32R)
        rel = at("rel", AR + 16 * K, [33, 6])
        toe = at("toe", AR + 17 * K, [2, NG * TOE])

        a_hi = at("a_hi", AR, [P, 2 * GT, S], F32R)
        a_lo = at("a_lo", AR + 16 * K, [P, 2 * GT, S], F32R)
        silu = at("silu", AR + 32 * K, [P, 2, S])
        glu = at("glu", AR + 40 * K, [P, 2, S])
        norm_bufs = [(at(f"sq{v}", sq_at, [P, 2, S]), at(f"acc{v}", sq_at + 8 * K, [P, S]),
                      at(f"rB{v}", sq_at + 12 * K, [P, S]), at(f"hf{v}", sq_at + 16 * K, [P, 2, S]))
                     for v, sq_at in enumerate((AR + 32 * K, AR))]

        pr_sq = at("pr_sq", AR + 56 * K, [P, S])
        pr_rs = at("pr_rs", AR + 60 * K, [P, S])
        pr_vT = at("pr_vT", AR + 64 * K, [P, S])

        o_sb = at("o_sb", AR, [P, 3, S])
        o_dil = at("o_dil", AR + 12 * K, [P, S])
        o_x = at("o_x", AR + 16 * K, [P, 2, S])
        sb_q = at("sb_q", AR + 24 * K, [P, 2, S])
        sb_k = at("sb_k", AR + 32 * K, [P, 2, S])
        sb_v = at("sb_v", AR + 40 * K, [P, 2, 8, P])
        sb_l = at("sb_l", XT, [P, 2, S])
        sb_sp = at("sb_sp", XT + 8 * K, [P, 2, S])
        sb_sum = at("sb_sum", XT + 16 * K, [P, 2, S])
        sb_a = at("sb_a", XT + 24 * K, [P, 2, S])
        d_qk = at("d_qk", XT, [P, 6, S])
        d_v = at("d_v", XT + 24 * K, [P, 2, 8, P])
        d_v2 = at("d_v2", AR + 32 * K, [P, 8, P])
        bias = at("bias", AR + 36 * K, [P, 2, STRIP])
        d_p = at("d_p", AR + 52 * K, [P, 2, STRIP])
        d_pT = at("d_pT", AR + 24 * K, [P, 3, 512])
        x_q = at("x_q", AR + 48 * K, [P, 2, S])
        x_p = at("x_p", AR + 24 * K, [P, 4, MEM])
        x_pT = at("x_pT", AR + 28 * K, [P, MB, 512])
        oM_hi = at("oM_hi", XT, [P, BR, S], F32R)
        oM_lo = at("oM_lo", AR + 24 * K, [P, BR, S], F32R)
        gate = at("gate", AR + 48 * K, [P, 3, S])
        merged = at("merged", AR, [P, 6, S])
        merged2 = at("merged2", XT + 24 * K, [P, 2, S])
        x_back = at("x_back", AR + 24 * K, [P, DT, S])
        y_nat = at("y_nat", AR, [P, 2, D])

        ps = ctx.enter_context(nc.psum_tensor("ps", [P, 4, 1024], F32))

        x_keep = nc.dram_tensor("x_keep", (P, DT * S), F32, kind="Internal").ap()
        toe_keep = nc.dram_tensor("toe_keep", (2, P, NG * TOE), F32, kind="Internal").ap()

        x_in = [sem(f"x_in{i}") for i in range(8)]
        mem_in, cst_in, gain_in, hgain_in = sem("mem_in"), sem("cst_in"), sem("gain_in"), sem("hgain_in")
        onehot_in, rel_in = sem("onehot_in"), sem("rel_in")
        consts_ready = sem("consts_ready")
        gains_ready = sem("gains_ready")
        raw_in = [sem(f"raw_in{i}") for i in range(NRAW)]
        hi_done, split_done, unit_done = sem("hi_done"), sem("split_done"), sem("unit_done")
        toe_done, toe_kept, toe_out, bias_in = sem("toe_done"), sem("toe_kept"), sem("toe_out"), [sem("bias_in0"), sem("bias_in1")]
        m_ss_done, m_rs_done, m_scaled = sem("m_ss_done"), sem("m_rs_done"), sem("m_scaled")
        m_turned, mT_done, mT_hi_done, mT_split = sem("m_turned"), sem("mT_done"), sem("mT_hi_done"), sem("mT_split")
        x_turned, xT_done = sem("x_turned"), sem("xT_done")
        sq_done, acc_done, ss_done = sem("sq_done"), sem("acc_done"), sem("ss_done")
        ln_done, rstd_done, newton = sem("ln_done"), sem("rstd_done"), sem("newton")
        hf_done, h_hi_done, h_ready = sem("hf_done"), sem("h_hi_done"), sem("h_ready")
        silu_done, glu_done, a_hi_done, a_ready = sem("silu_done"), sem("glu_done"), sem("a_hi_done"), sem("a_ready")
        down_done, down_added = sem("down_done"), sem("down_added")
        pr_copied, pr_sq_done = sem("pr_copied"), sem("pr_sq_done")
        pr_aux, pr_ln, pr_rstd, pr_newton, pr_final = (sem(f"pr_{n}") for n in ("aux", "ln", "rstd", "newton", "final"))
        x_kept, x_back_in = sem("x_kept"), sem("x_back_in")
        sb_z, sb_abs, sb_exp, sb_ln = sem("sb_z"), sem("sb_abs"), sem("sb_exp"), sem("sb_ln")
        sb_soft, sb_sp_ready, sb_sum_ready = sem("sb_soft"), sem("sb_sp_ready"), sem("sb_sum_ready")
        sb_cum, sb_a_ready, sb_av, sb_o = sem("sb_cum"), sem("sb_a_ready"), sem("sb_av"), sem("sb_o")
        d_z, d_biased, d_negmax, d_exp, d_rden, d_prob = (sem(f"d_{n}") for n in ("z", "biased", "negmax", "exp", "rden", "prob"))
        d_turned, d_pT_ready, d_pv, d_o, d_gap = (sem(f"d_{n}") for n in ("turned", "pT_ready", "pv", "o", "gap"))
        xa_z, xa_max, xa_sub, xa_exp, xa_sum, xa_rden, xa_prob = (
            sem(f"xa_{n}") for n in ("z", "max", "sub", "exp", "sum", "rden", "prob"))
        xa_turned, xa_pT, xa_pv, xa_o = (sem(f"xa_{n}") for n in ("turned", "pT", "pv", "o"))
        o_hi_done, o_split = sem("o_hi_done"), sem("o_split")
        gate_done, gated, gated_sum = sem("gate_done"), sem("gated"), sem("gated_sum")
        br_done = sem("br_done")
        mg_hi_done, mg_split = sem("mg_hi_done"), sem("mg_split")
        x_added = sem("x_added")
        y_turned, y_ready, y_out = sem("y_turned"), [sem("y_ready0"), sem("y_ready1")], [sem("y_out0"), sem("y_out1")]

        def after(eng, s, value):
            if not isinstance(value, int) or value > 0:
                eng.wait_ge(s, value)

        def at_turn(k, i, step=BODY):
            return k if i is None else step * i + k

        def o_tile(i):
            return o_sb[:, i, :] if i < 3 else o_dil[:, :] if i == 3 else o_x[:, i - 4, :]

        def merged_tile(m):
            return merged[:, m, :] if m < 6 else merged2[:, m - 6, :]

        def v_dil(g):
            return d_v[:, g] if g < 2 else d_v2

        def proj_dest(n):
            if n < 2:
                return mkT[:, n, :]
            if n < 4:
                return mv[:, :, (n - 2) * P:(n - 1) * P]
            if n < PR_QX:
                h = (n - PR_SB) // 3 % 2
                return (sb_q[:, h, :], sb_k[:, h, :], sb_v[:, h])[(n - PR_SB) % 3]
            if n < PR_DIL:
                return x_q[:, n - PR_QX, :]
            if n < PR_DIL + 6:
                return d_qk[:, n - PR_DIL, :]
            return v_dil(n - PR_DIL - 6)[:, :, :]

        def proj_gain(n):
            return 3 if n < 2 else 2 if n < PR_DIL else 0 if n < PR_DIL + 3 else 1

        def sum_count(s):
            head, i = divmod(s, 8)
            return head * 13 + (1 + 2 * i if i < 7 else 13)

        def bank(i):
            return ps[:, i // 2, (i % 2) * 512:(i % 2) * 512 + 512]

        def ps_flat(lo, hi):
            return ps[:, 0:2, :].rearrange("p a b -> p (a b)")[:, lo:hi]

        chunks = []
        for n in range(16):
            blocks = dilated_plan(n % 8)[1]
            chunks += [(n, blocks[c:c + 4], c == 0, c + 4 >= len(blocks)) for c in range(0, len(blocks), 4)]

        def chunks_before(n):
            return sum(c[0] < n for c in chunks)

        block = ctx.enter_context(nc.Block())

        @block.sync
        def _(sp):
            sp.dma_start(m_nat[:], mem.rearrange("(b p) d -> p b d", p=P)).then_inc(mem_in, 16)
            sp.dma_start(cst[:], consts).then_inc(cst_in, 16)
            sp.dma_start(oh[:], onehot).then_inc(onehot_in, 16)
            sp.dma_start(rel[0:32, :], rel_bias).then_inc(rel_in, 16)
            sp.dma_start(hg_raw[:], head_gains).then_inc(hgain_in, 16)
            sp.dma_start(g_raw[:], gains).then_inc(gain_in, 16)
            for b in range(8):
                sp.dma_start(x_nat[:, b, :], x[b * P:(b + 1) * P, :]).then_inc(x_in[b], 16)

            for r in range(NRAW):
                sp.dma_start(raw[:, r, :], weights[r]).then_inc(raw_in[r], 16)
            with sp.Fori(1, UNITS // NRAW) as i:
                for r in range(NRAW):
                    sp.wait_ge(split_done, NRAW * i + r - NRAW + 1)
                    sp.dma_start(raw[:, r, :], weights[bass.ds(NRAW * i + r, 1)].rearrange("a p n -> p (a n)")
                                 ).then_inc(raw_in[r], 16)
            for b in range(8):
                sp.wait_ge(y_ready[b % 2], b // 2 + 1)
                sp.dma_start(out[b * P:(b + 1) * P, :], y_nat[:, b % 2, :]).then_inc(y_out[b % 2], 16)
            sp.wait_ge(y_out[0], 64)
            sp.wait_ge(y_out[1], 64)

        @block.gpsimd
        def _(pool):
            for s in range(48):
                j = 7 - s % 8
                pool.wait_ge(sb_sp_ready, s + 1)
                if j == 0:
                    continue
                if s:
                    pool.wait_ge(sb_cum, s)
                    pool.wait_ge(sb_sum_ready, sum_count(s - 1))
                a, b = j * P, (j + 1) * P
                nc.gpsimd.tensor_copy(sb_sum[:, (s + 1) % 2, a:b], sb_sp[:, s % 2, a:b]).then_inc(sb_sum_ready, 1)
                if j < 7:
                    nc.gpsimd.tensor_tensor(sb_sum[:, (s + 1) % 2, b:], sb_sum[:, s % 2, b:], sb_sp[:, s % 2, b:],
                                            ALU.add).then_inc(sb_sum_ready, 1)

        @block.scalar
        def _(act):
            def split_hi(k, i=None):
                if i is None and k >= UNITS:
                    return
                act.wait_ge(raw_in[k % NRAW], 16 * (at_turn(k // NRAW, i, BODY // NRAW) + 1))
                after(act, unit_done, at_turn(k, i) - NW + 1)
                nc.scalar.activation(w_hi[:, k % NW].rearrange("p a b -> p (a b)"), raw[:, k % NRAW, :],
                                     ACT.Copy).then_inc(hi_done, 1)

            def square(r, k):
                sq, acc, rB, hf = norm_bufs[r // 2]
                if k > 2:
                    act.wait_ge(acc_done, 7 * r + k - 2)
                nc.scalar.activation(sq[:, k % 2, :] if k else acc[:], xT[:, k, :], ACT.Square).then_inc(sq_done, 1)

            def norm(r):
                sq, acc, rB, hf = norm_bufs[r // 2]
                act.wait_ge(ss_done, r + 1)
                nc.scalar.activation(rB[:], ps[:, 0, :], ACT.Ln, bias=eps_d[:, 0:1]).then_inc(ln_done, 1)
                act.wait_ge(ln_done, r + 1)
                nc.scalar.activation(rB[:], rB[:], ACT.Exp, scale=-0.5).then_inc(rstd_done, 1)
                act.wait_ge(rstd_done, 2 * r + 1)
                nc.scalar.activation(sq[:, 0, :], rB[:], ACT.Square).then_inc(rstd_done, 1)
                for k in range(DT):
                    act.wait_ge(hf_done, 8 * r + k + 1)
                    nc.scalar.activation(h_hi[:, k, :], hf[:, k % 2, :], ACT.Copy).then_inc(h_hi_done, 1)

            def ffn_tile(k, t, i=None):
                split_hi(k + AHEAD, i)
                act.wait_ge(unit_done, at_turn(k, i) + 1)
                after(act, glu_done, at_turn(t, i, 2 * GT) - 1)
                nc.scalar.activation(silu[:, t % 2, :], ps[:, 0, :], ACT.Silu).then_inc(silu_done, 1)
                split_hi(k + 1 + AHEAD, i)

            def ffn(f, u0):
                t0, u1 = FT * f, u0 + 2 * GT
                for q in range(GT):
                    ffn_tile(u0 + 2 * q, t0 + q)
                with act.Fori(0, (NGRP - 1) // 2) as i:
                    for half in range(2):
                        k = u1 + 3 * GT * half
                        for q in range(GT):
                            ffn_tile(k + 2 * q, t0 + GT * (1 + half) + q, i)
                        for q in range(GT):
                            split_hi(k + 2 * GT + q + AHEAD, i)
                for q in range(GT - 1):
                    split_hi(u0 + FFN_UNITS - GT + q + AHEAD)

            def proj_square(n):
                kind, w = PROJ[n]
                if kind == "norm":
                    act.wait_ge(pr_copied, n + 1)
                    after(act, pr_final, aux_before(n))
                    nc.scalar.activation(pr_sq[:, 0:w], proj_dest(n), ACT.Square).then_inc(pr_sq_done, 1)

            def proj_rstd(n):
                kind, w = PROJ[n]
                if kind == "norm":
                    i = count_before(("norm",), n)
                    act.wait_ge(pr_aux, aux_before(n) + 1)
                    nc.scalar.activation(pr_rs[:, 0:w], ps[:, aux_pair(n), 0:w], ACT.Ln, bias=eps_h[:, 0:1]).then_inc(pr_ln, 1)
                    act.wait_ge(pr_ln, i + 1)
                    nc.scalar.activation(pr_rs[:, 0:w], pr_rs[:, 0:w], ACT.Exp, scale=-0.5).then_inc(pr_rstd, 1)
                    act.wait_ge(pr_rstd, 2 * i + 1)
                    nc.scalar.activation(pr_sq[:, 0:w], pr_rs[:, 0:w], ACT.Square).then_inc(pr_rstd, 1)

            def projections(n0, n1):
                for n in range(n0, n1):
                    split_hi(proj_unit(n) + AHEAD)
                    if n > n0:
                        proj_rstd(n - 1)
                    proj_square(n)
                proj_rstd(n1 - 1)

            act.preload_act_table_set("natural_log_exp_and_others")
            act.wait_ge(mem_in, 16)
            for b in range(MB):
                if b:
                    act.wait_ge(m_ss_done, b)
                nc.scalar.activation(m_sq[:], m_nat[:, b, :], ACT.Square, accum_out=m_ss[:, b:b + 1]).then_inc(m_ss_done, 1)
            act.wait_ge(m_ss_done, MB)
            act.wait_ge(consts_ready, 2)
            nc.scalar.activation(m_rs[:], m_ss[:], ACT.Ln, bias=eps_d[:, 0:1]).then_inc(m_rs_done, 1)
            act.wait_ge(m_rs_done, 1)
            nc.scalar.activation(m_rs[:], m_rs[:], ACT.Exp, scale=-0.5).then_inc(m_rs_done, 1)
            act.wait_ge(toe_kept, NG + 1)
            for hh in range(2):
                act.dma_start(toe_keep[hh:hh + 1, :, :], toe[hh:hh + 1, :].unsqueeze(1).to_broadcast([1, P, NG * TOE])
                              ).then_inc(toe_out, 16)
            for k in range(DT):
                act.wait_ge(mT_done, k + 1)
                nc.scalar.activation(mT_hi[:, k, :], mT[:, k, :], ACT.Copy).then_inc(mT_hi_done, 1)
            split_hi(0)
            split_hi(1)
            projections(0, PR_SB)

            act.wait_ge(xT_done, 8)
            for k in range(DT):
                square(0, k)
            norm(0)
            ffn(0, U_FFN1)
            act.preload_act_table_set("natural_log_exp_and_others")
            for k in range(DT):
                act.wait_ge(down_added, DT * (NGRP - 1) + k + 1)
                square(1, k)
            split_hi(U_FFN1 + FFN_UNITS - 1 + AHEAD)
            norm(1)
            act.wait_ge(h_ready, 16)
            act.dma_start(x_keep[:, :], xT[:, :, :].rearrange("p k s -> p (k s)")).then_inc(x_kept, 16)

            def load_bias(hh):
                for g, c, w, x0 in dilated_windows():
                    src = bass.AP(toe_keep.tensor, (hh * P * NG + g) * TOE + x0, [[NG * TOE - 1, P], [1, w]])
                    act.dma_start(bias[:, hh, c:c + w], src).then_inc(bias_in[hh], 16)

            def d_evacuate(c):
                w = len(chunks[c][1]) * P
                act.wait_ge(d_turned, c + 1)
                after(act, d_pv, c - 2)
                nc.scalar.activation(d_pT[:, c % 3, 0:w], bank(4 + c % 3)[:, 0:w], ACT.Copy).then_inc(d_pT_ready, 1)

            def sb_explog(s):
                a = (7 - s % 8) * P
                act.wait_ge(sb_z, s + 1)
                after(act, sb_sp_ready, s - 1)
                nc.scalar.activation(sb_l[:, s % 2, a:], ps[:, s % 2, a:], ACT.Abs).then_inc(sb_abs, 1)
                act.wait_ge(sb_abs, s + 1)
                nc.scalar.activation(sb_l[:, s % 2, a:], sb_l[:, s % 2, a:], ACT.Exp, scale=-1.0).then_inc(sb_exp, 1)
                act.wait_ge(sb_exp, s + 1)
                nc.scalar.activation(sb_l[:, s % 2, a:], sb_l[:, s % 2, a:], ACT.Ln, bias=1.0).then_inc(sb_ln, 1)

            def sb_weights(s):
                a = (7 - s % 8) * P
                act.wait_ge(sb_cum, s + 1)
                after(act, sb_av, s - 1)
                nc.scalar.activation(sb_a[:, s % 2, a:], ps[:, s % 2, a:], ACT.Exp).then_inc(sb_a_ready, 1)

            projections(PR_SB, PR_BESIDE)
            for pair in range(3):
                beside = beside_sb(pair)
                for s in range(16):
                    f, phase = divmod(s, SB_EVERY)
                    if phase == 0:
                        if f:
                            if f <= len(beside):
                                proj_rstd(beside[f - 1])
                        if f < len(beside):
                            split_hi(proj_unit(beside[f]) + AHEAD)
                    sb_explog(16 * pair + s)
                    if s:
                        sb_weights(16 * pair + s - 1)
                    if phase == SB_EVERY - 1 and f < len(beside):
                        proj_square(beside[f])
                sb_weights(16 * pair + 15)

            act.wait_ge(sb_o, 6)
            act.wait_ge(toe_out, 32)
            load_bias(0)

            for n in range(10):
                p = PR_DIL + n
                if n < 8:
                    act.wait_ge(xa_sub, n + 1)
                    nc.scalar.activation(x_p[:], x_p[:], ACT.Exp).then_inc(xa_exp, 1)
                if n:
                    proj_square(p - 1)
                if n < 9:
                    split_hi(proj_unit(p) + AHEAD)
                if n < 8:
                    for b in range(MB):
                        act.wait_ge(xa_turned, 2 * n + b + 1)
                        after(act, xa_pv, n)
                        nc.scalar.activation(x_pT[:, b, :], ps[:, 1, 512 * b:512 * b + 512], ACT.Copy).then_inc(xa_pT, 1)
                if n:
                    proj_rstd(p - 1)
            act.wait_ge(xa_o, 8)
            load_bias(1)

            at_chunk = 0
            for n in range(16):
                segs, blocks = dilated_plan(n % 8)
                lo, hi = segs[0][0], segs[-1][1]
                act.wait_ge(d_negmax, n + 1)
                after(act, d_rden, n)
                nc.scalar.activation(d_p[:, n % 2, lo:hi], d_p[:, n % 2, lo:hi], ACT.Exp, bias=b_nmax[:, 0:1],
                                     accum_out=b_den[:, 0:1]).then_inc(d_exp, 1)
                for c in range(chunks_before(n - 1), chunks_before(n)) if n else ():
                    d_evacuate(c)
            for c in range(chunks_before(15), len(chunks)):
                d_evacuate(c)

            act.wait_ge(d_o, 4)
            for i in range(BR):
                nc.scalar.activation(oM_hi[:, i, :], o_tile(i), ACT.Copy).then_inc(o_hi_done, 1)
            for m in range(DT):
                u = U_MERGE + 4 * m
                for b in range(3):
                    split_hi(u + b + AHEAD)
                    act.wait_ge(unit_done, u + b + 1)
                    if b:
                        after(act, gated_sum, 2 * (m - 1) + b)
                    else:
                        after(act, gated, 3 * (m - 1) + 1)
                    nc.scalar.activation(gate[:, b, :], ps[:, b, :], ACT.Sigmoid).then_inc(gate_done, 1)
                split_hi(u + 3 + AHEAD)

            act.wait_ge(gated_sum, 16)
            act.dma_start(x_back[:, :, :].rearrange("p k s -> p (k s)"), x_keep[:, :]).then_inc(x_back_in, 16)
            for m in range(DT):
                nc.scalar.activation(h_hi[:, m, :], merged_tile(m), ACT.Copy).then_inc(mg_hi_done, 1)
            act.preload_act_table_set("natural_log_exp_and_others")
            for m in range(DT):
                split_hi(U_OUT + m + AHEAD)
                act.wait_ge(x_added, m + 1)
                square(2, m)
            norm(2)
            ffn(1, U_FFN2)

            for b in range(0, 8, 2):
                act.wait_ge(y_turned, b + 1)
                after(act, y_out[0], 16 * (b // 2))
                nc.scalar.activation(y_nat[:, 0, :], ps[:, 0, :], ACT.Copy).then_inc(y_ready[0], 1)

        def d_out(dve, n):
            hh, b = divmod(n, 8)
            dve.wait_ge(d_pv, chunks_before(n + 1))
            nc.vector.tensor_copy(o_dil[hh * HD:hh * HD + HD, (b - 3) * P:(b + 1) * P],
                                  bank(7)[hh * HD:hh * HD + HD, :]).then_inc(d_o, 1)

        @block.vector
        def _(dve):
            def split_lo(k, i=None):
                if i is None and k >= UNITS:
                    return
                dve.wait_ge(hi_done, at_turn(k, i) + 1)
                nc.vector.tensor_tensor(w_lo[:, k % NW].rearrange("p a b -> p (a b)"), raw[:, k % NRAW, :],
                                        w_hi[:, k % NW].rearrange("p a b -> p (a b)").bitcast(F32),
                                        ALU.subtract).then_inc(split_done, 1)

            def square_sum(r, k):
                sq, acc, rB, hf = norm_bufs[r // 2]
                dve.wait_ge(sq_done, 8 * r + k + 1)
                if k > 1:
                    dve.wait_ge(acc_done, 7 * r + k - 1)
                nc.vector.tensor_tensor(acc[:], acc[:], sq[:, k % 2, :], ALU.add).then_inc(acc_done, 1)

            def norm_rest(r, gain):
                sq, acc, rB, hf = norm_bufs[r // 2]
                dve.wait_ge(rstd_done, 2 * r + 2)
                nc.vector.scalar_tensor_tensor(out=sq[:, 0, :], in0=ps[:, 0, :], scalar=D * EPS, in1=sq[:, 0, :],
                                               op0=ALU.add, op1=ALU.mult).then_inc(newton, 1)
                dve.wait_ge(newton, 3 * r + 1)
                nc.vector.tensor_scalar(sq[:, 0, :], sq[:, 0, :], -0.5, 1.5, ALU.mult, ALU.add).then_inc(newton, 1)
                dve.wait_ge(newton, 3 * r + 2)
                nc.vector.tensor_tensor(rB[:], rB[:], sq[:, 0, :], ALU.mult).then_inc(newton, 1)
                dve.wait_ge(newton, 3 * r + 3)
                for k in range(DT + 1):
                    if k < DT:
                        if k > 1:
                            dve.wait_ge(h_ready, 8 * r + k - 1)
                        nc.vector.scalar_tensor_tensor(out=hf[:, k % 2, :], in0=xT[:, k, :], scalar=g32[:, gain, k:k + 1],
                                                       in1=rB[:], op0=ALU.mult, op1=ALU.mult).then_inc(hf_done, 1)
                    if k:
                        dve.wait_ge(h_hi_done, 8 * r + k)
                        nc.vector.tensor_tensor(h_lo[:, k - 1, :], hf[:, (k - 1) % 2, :],
                                                h_hi[:, k - 1, :].bitcast(F32), ALU.subtract).then_inc(h_ready, 1)

            def glu_tile(k, t, slot, i=None):
                split_lo(k - 1 + AHEAD, i)
                split_lo(k + AHEAD, i)
                count = at_turn(t, i, 2 * GT)
                dve.wait_ge(unit_done, at_turn(k, i) + 1)
                dve.wait_ge(silu_done, count + 1)
                after(dve, a_ready, count - 1)
                nc.vector.scalar_tensor_tensor(out=glu[:, t % 2, :], in0=silu[:, t % 2, :], scalar=0.5, in1=ps[:, 1, :],
                                               op0=ALU.mult, op1=ALU.mult).then_inc(glu_done, 1)
                dve.wait_ge(glu_done, count + 1)
                nc.vector.tensor_copy(a_hi[:, slot, :], glu[:, t % 2, :]).then_inc(a_hi_done, 1)
                dve.wait_ge(a_hi_done, count + 1)
                nc.vector.tensor_tensor(a_lo[:, slot, :], glu[:, t % 2, :], a_hi[:, slot, :].bitcast(F32),
                                        ALU.subtract).then_inc(a_ready, 1)

            def add_down(g, k, i=None, finish=None):
                for m in range(DT):
                    if m == 2:
                        split_lo(k - 1 + AHEAD, i)
                    if m < DT - 1:
                        dve.wait_ge(down_done, at_turn((DT - 1) * g + m + 1, i, 2 * (DT - 1)))
                    else:
                        dve.wait_ge(unit_done, at_turn(k + 1, i))
                    nc.vector.tensor_tensor(xT[:, m, :], xT[:, m, :], ps[:, 2 + m % 2, :], ALU.add).then_inc(down_added, 1)
                    if finish:
                        finish(m)
                split_lo(k + AHEAD, i)

            def ffn(f, u0, finish=None):
                t0, g0, u1 = FT * f, NGRP * f, u0 + 2 * GT
                for q in range(GT):
                    glu_tile(u0 + 2 * q + 1, t0 + q, q)
                with dve.Fori(0, (NGRP - 1) // 2) as i:
                    for half in range(2):
                        k = u1 + 3 * GT * half
                        for q in range(GT):
                            glu_tile(k + 2 * q + 1, t0 + GT * (1 + half) + q, GT * (1 - half) + q, i)
                        add_down(g0 + half, k + 3 * GT - 1, i)
                add_down(g0 + NGRP - 1, u0 + FFN_UNITS - 1, None, finish)

            def proj_copy(n):
                kind, w = PROJ[n]
                dve.wait_ge(unit_done, proj_unit(n) + 1)
                src = ps[:, proj_pair(n), 0:w]
                if kind == "turn":
                    after(dve, pr_aux, aux_before(n))
                    nc.vector.tensor_copy(pr_vT[:, 0:w], src).then_inc(pr_copied, 1)
                elif kind == "copy" and (n - PR_SB) % 3 == 0:
                    nc.vector.tensor_scalar(proj_dest(n), src, HD ** -0.5, None, ALU.mult).then_inc(pr_copied, 1)
                else:
                    nc.vector.tensor_copy(proj_dest(n), src).then_inc(pr_copied, 1)

            def proj_final(n):
                kind, w = PROJ[n]
                i, a = count_before(("norm",), n), aux_before(n)
                src = ps[:, aux_pair(n), 0:w]
                if kind == "norm":
                    dve.wait_ge(pr_rstd, 2 * i + 2)
                    nc.vector.scalar_tensor_tensor(out=pr_sq[:, 0:w], in0=src, scalar=HD * EPS, in1=pr_sq[:, 0:w],
                                                   op0=ALU.add, op1=ALU.mult).then_inc(pr_newton, 1)
                    c = proj_gain(n)
                    nc.vector.scalar_tensor_tensor(out=proj_dest(n), in0=proj_dest(n), scalar=hg[:, c:c + 1],
                                                   in1=pr_rs[:, 0:w], op0=ALU.mult, op1=ALU.mult).then_inc(pr_newton, 1)
                    dve.wait_ge(pr_newton, 3 * i + 2)
                    nc.vector.tensor_scalar(pr_sq[:, 0:w], pr_sq[:, 0:w], -0.5, 1.5, ALU.mult, ALU.add).then_inc(pr_newton, 1)
                    dve.wait_ge(pr_newton, 3 * i + 3)
                    nc.vector.tensor_tensor(proj_dest(n), proj_dest(n), pr_sq[:, 0:w], ALU.mult).then_inc(pr_final, 1)
                elif kind == "turn":
                    dve.wait_ge(pr_aux, a + 1)
                    nc.vector.tensor_copy(proj_dest(n), src.rearrange("p (b c) -> p b c", c=P)).then_inc(pr_final, 1)

            def projections(n0, n1):
                for n in range(n0, n1):
                    split_lo(proj_unit(n) + AHEAD)
                    if n > n0:
                        proj_final(n - 1)
                    proj_copy(n)
                proj_final(n1 - 1)

            nc.vector.memset(eps_d[:], D * EPS).then_inc(consts_ready, 1)
            nc.vector.memset(eps_h[:], HD * EPS).then_inc(consts_ready, 1)
            nc.vector.memset(rel[32:33, :], NEG).then_inc(consts_ready, 1)
            dve.wait_ge(gain_in, 16)
            nc.vector.tensor_scalar(g32[:], g_raw[:], float(D) ** 0.5, None, ALU.mult).then_inc(gains_ready, 1)
            dve.wait_ge(hgain_in, 16)
            nc.vector.tensor_scalar(hg[:, 0:1], hg_raw[:, 0:1], 1.0, None, ALU.mult).then_inc(gains_ready, 1)
            nc.vector.tensor_scalar(hg[:, 1:2], hg_raw[:, 1:2], 8.0, None, ALU.mult).then_inc(gains_ready, 1)
            nc.vector.tensor_scalar(hg[:, 2:3], hg_raw[:, 2:3], 1.0, None, ALU.mult).then_inc(gains_ready, 1)
            nc.vector.tensor_scalar(hg[:, 3:4], hg_raw[:, 3:4], 8.0, None, ALU.mult).then_inc(gains_ready, 1)
            dve.wait_ge(gains_ready, 5)
            dve.wait_ge(m_rs_done, 2)
            for b in range(MB):
                nc.vector.tensor_scalar(m_nat[:, b, :], m_nat[:, b, :], m_rs[:, b:b + 1], None, ALU.mult).then_inc(m_scaled, 1)
            for q in range(NG):
                dve.wait_ge(toe_done, q + 1)
                nc.vector.tensor_copy(toe[:, q * TOE:q * TOE + 1024], ps[0:2, q, :]).then_inc(toe_kept, 1)
            nc.vector.tensor_copy(toe[:, :].rearrange("p (g n) -> p g n", g=NG)[:, :, 1024:TOE],
                                  ps[0:2, 3, 0:NG * P].rearrange("p (g n) -> p g n", g=NG)).then_inc(toe_kept, 1)
            for k in range(DT):
                dve.wait_ge(m_turned, k // 4 + 1)
                nc.vector.tensor_scalar(mT[:, k, :], ps[:, k // 4, (k % 4) * MEM:(k % 4 + 1) * MEM],
                                        g32[:, 3, k:k + 1], None, ALU.mult).then_inc(mT_done, 1)
            for k in range(DT):
                dve.wait_ge(mT_hi_done, k + 1)
                nc.vector.tensor_tensor(mT_lo[:, k, :], mT[:, k, :], mT_hi[:, k, :].bitcast(F32),
                                        ALU.subtract).then_inc(mT_split, 1)
            split_lo(0)
            split_lo(1)
            projections(0, PR_SB)
            for b in range(8):
                dve.wait_ge(x_turned, b + 1)
                nc.vector.tensor_copy(xT[:, :, b * P:(b + 1) * P], ps[:, b % 2, :].rearrange("p (k s) -> p k s", s=P)
                                      ).then_inc(xT_done, 1)
            for k in range(1, DT):
                square_sum(0, k)
            norm_rest(0, 0)
            dve.wait_ge(toe_out, 32)
            ffn(0, U_FFN1, lambda m: square_sum(1, m - 1) if m > 1 else None)
            square_sum(1, DT - 1)
            norm_rest(1, 1)

            def x_subtract(n):
                z = ps[:, 0, :].rearrange("p (b m) -> p b m", b=4)
                dve.wait_ge(xa_z, n + 1)
                after(dve, xa_prob, n)
                nc.vector.tensor_reduce(x_max[:], z, AX.X, ALU.max).then_inc(xa_max, 1)
                dve.wait_ge(xa_max, n + 1)
                after(dve, xa_turned, 2 * n)
                nc.vector.tensor_tensor(x_p[:], z, x_max[:].unsqueeze(2).to_broadcast([P, 4, MEM]),
                                        ALU.subtract).then_inc(xa_sub, 1)

            def x_divide(n):
                dve.wait_ge(xa_exp, n + 1)
                nc.vector.tensor_reduce(x_den[:], x_p[:], AX.X, ALU.add).then_inc(xa_sum, 1)
                dve.wait_ge(xa_sum, n + 1)
                nc.vector.reciprocal(x_rden[:], x_den[:]).then_inc(xa_rden, 1)
                dve.wait_ge(xa_rden, n + 1)
                nc.vector.tensor_tensor(x_p[:], x_p[:], x_rden[:].unsqueeze(2).to_broadcast([P, 4, MEM]),
                                        ALU.mult).then_inc(xa_prob, 1)

            def sb_softplus(s):
                a = (7 - s % 8) * P
                dve.wait_ge(sb_ln, s + 1)
                if s >= 2:
                    dve.wait_ge(sb_cum, s - 1)
                    dve.wait_ge(sb_sum_ready, sum_count(s - 2))
                nc.vector.scalar_tensor_tensor(out=sb_sp[:, s % 2, a:], in0=ps[:, s % 2, a:], scalar=0.0,
                                               in1=sb_l[:, s % 2, a:], op0=ALU.max, op1=ALU.add).then_inc(sb_soft, 1)
                dve.wait_ge(sb_soft, s + 1)
                nc.vector.tensor_tensor(sb_sp[:, s % 2, a:a + P], sb_sp[:, s % 2, a:a + P], causal,
                                        ALU.mult).then_inc(sb_sp_ready, 1)

            def sb_out(head):
                r = (head % 2) * HD
                dve.wait_ge(sb_av, 8 * head + 8)
                nc.vector.tensor_copy(o_sb[r:r + HD, head // 2, :], ps[r:r + HD, 2, :]).then_inc(sb_o, 1)

            dve.wait_ge(x_kept, 16)
            projections(PR_SB, PR_BESIDE)
            for pair in range(3):
                beside = beside_sb(pair)
                for s in range(16):
                    f, phase = divmod(s, SB_EVERY)
                    if phase == 0 and f < len(beside):
                        split_lo(proj_unit(beside[f]) + AHEAD)
                    sb_softplus(16 * pair + s)
                    if phase == 0 and 0 < f <= len(beside):
                        proj_final(beside[f - 1])
                    if phase == SB_EVERY - 1 and f < len(beside):
                        proj_copy(beside[f])
                    if s == 8:
                        sb_out(2 * pair)
                sb_out(2 * pair + 1)

            for n in range(10):
                p = PR_DIL + n
                if n < 8:
                    x_subtract(n)
                if n:
                    proj_copy(p - 1)
                if 0 < n < 9:
                    h, half = divmod(n - 1, 2)
                    r = (h % 2) * HD
                    dve.wait_ge(xa_pv, n)
                    nc.vector.tensor_copy(o_x[r:r + HD, h // 2, 512 * half:512 * half + 512],
                                          bank(2)[r:r + HD, :]).then_inc(xa_o, 1)
                if n < 8:
                    x_divide(n)
                if n < 9:
                    split_lo(proj_unit(p) + AHEAD)
                if n:
                    proj_final(p - 1)

            gap_done = 0
            for n in range(16):
                hh, b = divmod(n, 8)
                segs, blocks = dilated_plan(b)
                lo, hi = segs[0][0], segs[-1][1]
                if b == 0:
                    dve.wait_ge(bias_in[hh], 16 * 7)
                dve.wait_ge(d_z, n + 1)
                if n > 1:
                    dve.wait_ge(d_turned, chunks_before(n - 1))
                if n:
                    dve.wait_ge(d_exp, n)
                if len(segs) == 1:
                    nc.vector.tensor_tensor_reduce(d_p[:, n % 2, lo:hi], ps_flat(lo, hi), bias[:, hh, lo:hi], 1.0, -3e38,
                                                   ALU.add, ALU.max, b_max[:, 0:1]).then_inc(d_biased, 1)
                else:
                    for c, d in segs:
                        nc.vector.tensor_tensor(d_p[:, n % 2, c:d], ps_flat(c, d), bias[:, hh, c:d], ALU.add).then_inc(d_gap, 1)
                    nc.vector.memset(d_p[:, n % 2, segs[0][1]:segs[1][0]], NEG).then_inc(d_gap, 1)
                    gap_done += 3
                    dve.wait_ge(d_gap, gap_done)
                    nc.vector.tensor_reduce(b_max[:, 0:1], d_p[:, n % 2, lo:hi], AX.X, ALU.max).then_inc(d_biased, 1)
                dve.wait_ge(d_biased, n + 1)
                nc.vector.tensor_scalar(b_nmax[:], b_max[:], -1.0, None, ALU.mult).then_inc(d_negmax, 1)
                dve.wait_ge(d_exp, n + 1)
                after(dve, d_prob, n)
                nc.vector.reciprocal(b_rden[:], b_den[:]).then_inc(d_rden, 1)
                dve.wait_ge(d_rden, n + 1)
                nc.vector.tensor_scalar(d_p[:, n % 2, lo:hi], d_p[:, n % 2, lo:hi], b_rden[:, 0:1], None,
                                        ALU.mult).then_inc(d_prob, 1)
                if n % 4 == 1 and n > 1:
                    d_out(dve, n - 2)
            d_out(dve, 15)

            for i in range(BR):
                dve.wait_ge(o_hi_done, i + 1)
                nc.vector.tensor_tensor(oM_lo[:, i, :], o_tile(i), oM_hi[:, i, :].bitcast(F32),
                                        ALU.subtract).then_inc(o_split, 1)
            for m in range(DT):
                u = U_MERGE + 4 * m
                for q in range(4):
                    split_lo(u + q + AHEAD)
                for b in range(3):
                    pair = (3, 0, 1)[b]
                    dve.wait_ge(gate_done, 3 * m + b + 1)
                    if b < 2:
                        dve.wait_ge(br_done, 2 * m + b + 1)
                    else:
                        dve.wait_ge(unit_done, u + 4)
                    to = merged_tile(m) if b == 0 else gate[:, b, :]
                    nc.vector.tensor_tensor(to, gate[:, b, :], ps[:, pair, :], ALU.mult).then_inc(gated, 1)
                for b in range(1, 3):
                    dve.wait_ge(gated, 3 * m + 3)
                    if b == 2:
                        dve.wait_ge(gated_sum, 2 * m + 1)
                    nc.vector.tensor_tensor(merged_tile(m), merged_tile(m), gate[:, b, :], ALU.add).then_inc(gated_sum, 1)

            for m in range(DT):
                dve.wait_ge(mg_hi_done, m + 1)
                nc.vector.tensor_tensor(h_lo[:, m, :], merged_tile(m), h_hi[:, m, :].bitcast(F32),
                                        ALU.subtract).then_inc(mg_split, 1)
            dve.wait_ge(x_back_in, 16)
            dve.wait_ge(mg_split, DT)
            for m in range(DT):
                split_lo(U_OUT + m + AHEAD)
                dve.wait_ge(unit_done, U_OUT + m + 1)
                nc.vector.tensor_tensor(xT[:, m, :], x_back[:, m, :], ps[:, 2 + m % 2, :], ALU.add).then_inc(x_added, 1)
                if m > 1:
                    square_sum(2, m - 1)
            square_sum(2, DT - 1)
            norm_rest(2, 2)
            ffn(1, U_FFN2)

            for b in range(1, 8, 2):
                dve.wait_ge(y_turned, b + 1)
                after(dve, y_out[1], 16 * (b // 2))
                nc.vector.tensor_copy(y_nat[:, 1, :], ps[:, 1, :]).then_inc(y_ready[1], 1)

        @block.tensor
        def _(pe):
            def mm(o, a, b, start, stop):
                return pe.matmul(o, a, b, start=start, stop=stop, skip_group_check=True)

            def product(pair, slot, hi, lo, width, tiles=DT, w0=0, there=None, k0=0, k1=None):
                halves = [(c, min(c + 512, width)) for c in range(0, width, 512)]
                for k in range(k0, tiles if k1 is None else k1):
                    if there:
                        there(k)
                    first, final = k == 0, k == tiles - 1
                    for c, d in halves:
                        mm(ps[:, pair, c:d], w_hi[:, slot, w0 + k, :], hi(k)[:, c:d], first, False)
                        mm(ps[:, pair, c:d], w_hi[:, slot, w0 + k, :], lo(k)[:, c:d], False, False)
                    for c, d in halves:
                        last = mm(ps[:, pair, c:d], w_lo[:, slot, w0 + k, :], hi(k)[:, c:d], False, final)
                return last

            def hh(k):
                return h_hi[:, k, :]

            def hl(k):
                return h_lo[:, k, :]

            def gate_up(k, t, i=None, there=None):
                for part in range(2):
                    pe.wait_ge(split_done, at_turn(k, i) + part + 1)
                    after(pe, (silu_done, glu_done)[part], at_turn(t, i, 2 * GT))
                    product(part, (k + part) % NW, hh, hl, S, there=there if part == 0 else None).then_inc(unit_done, 1)

            def down(g, k, slot, i=None):
                pe.wait_ge(split_done, at_turn(k, i) + GT)
                pe.wait_ge(a_ready, at_turn(GT * g, i, 2 * GT) + GT)
                for m in range(DT):
                    pair = 2 + m % 2
                    if m >= 2 or i is None:
                        pe.wait_ge(down_added, at_turn(DT * g, i, 2 * DT) + m - 1)
                    for q in range(GT):
                        s = (k + q) % NW
                        for c in (0, 512):
                            mm(ps[:, pair, c:c + 512], w_hi[:, s, m, :], a_hi[:, slot + q, c:c + 512], q == 0, False)
                            mm(ps[:, pair, c:c + 512], w_hi[:, s, m, :], a_lo[:, slot + q, c:c + 512], False, False)
                        for c in (0, 512):
                            last = mm(ps[:, pair, c:c + 512], w_lo[:, s, m, :], a_hi[:, slot + q, c:c + 512], False, q == GT - 1)
                    if m < DT - 1:
                        last.then_inc(down_done, 1)
                    else:
                        last.then_inc(unit_done, GT)

            def ffn(f, u0, r):
                t0, g0, u1 = FT * f, NGRP * f, u0 + 2 * GT
                gate_up(u0, t0, there=lambda k: pe.wait_ge(h_ready, 8 * r + k + 1))
                for q in range(1, GT):
                    gate_up(u0 + 2 * q, t0 + q)
                with pe.Fori(0, (NGRP - 1) // 2) as i:
                    for half in range(2):
                        k = u1 + 3 * GT * half
                        for q in range(GT):
                            gate_up(k + 2 * q, t0 + GT * (1 + half) + q, i)
                        down(g0 + half, k + 2 * GT, GT * half, i)
                down(g0 + NGRP - 1, u0 + FFN_UNITS - GT, 0)

            def norm_sum(r):
                acc = norm_bufs[r // 2][1]
                pe.wait_ge(acc_done, 7 * r + 7)
                for c in (0, 512):
                    last = mm(ps[:, 0, c:c + 512], ones, acc[:, c:c + 512], True, True)
                last.then_inc(ss_done, 1)

            def proj(n, hi, lo, there=None, k0=0, k1=DT):
                kind, w = PROJ[n]
                if k0 == 0:
                    pe.wait_ge(split_done, proj_unit(n) + 1)
                    if n < PR_BESIDE:
                        after(pe, pr_copied, n - 1)
                    else:
                        before = n if n < PR_DIL else n - 1
                        pe.wait_ge(pr_copied, before)
                        pe.wait_ge(pr_final, aux_before(before))
                last = product(proj_pair(n), proj_unit(n) % NW, hi, lo, w, there=there, k0=k0, k1=k1)
                if k1 == DT:
                    last.then_inc(unit_done, 1)

            def proj_aux(n):
                kind, w = PROJ[n]
                i, a, to = count_before(("norm",), n), aux_before(n), aux_pair(n)
                if kind == "norm":
                    pe.wait_ge(pr_sq_done, i + 1)
                elif kind == "turn":
                    pe.wait_ge(pr_copied, n + 1)
                if kind != "copy":
                    after(pe, pr_final, a)
                if kind == "norm":
                    for c in range(0, w, 512):
                        d = min(w, c + 512)
                        last = mm(ps[:, to, c:d], head_ones, pr_sq[:, c:d], True, True)
                    last.then_inc(pr_aux, 1)
                elif kind == "turn":
                    for b in range(w // P):
                        last = pe.transpose(ps[:, to, b * P:(b + 1) * P], pr_vT[:, b * P:(b + 1) * P], ident)
                    last.then_inc(pr_aux, 1)

            def projections(n0, n1, hi, lo, there=None):
                for n in range(n0, n1):
                    proj(n, hi, lo, there if n == n0 else None)
                    if n > n0:
                        proj_aux(n - 1)
                proj_aux(n1 - 1)

            pe.wait_ge(onehot_in, 16)
            pe.wait_ge(rel_in, 16)
            pe.wait_ge(consts_ready, 3)
            for g in range(NG):
                for c in (0, 512):
                    mm(ps[0:2, g, c:c + 512], rel[:, 2 * g:2 * g + 2], oh[:, g * TOE + c:g * TOE + c + 512], True, True)
                last = mm(ps[0:2, 3, g * P:(g + 1) * P], rel[:, 2 * g:2 * g + 2],
                          oh[:, g * TOE + 1024:(g + 1) * TOE], True, True)
                last.then_inc(toe_done, 1)
            pe.wait_ge(toe_kept, NG + 1)
            pe.wait_ge(cst_in, 16)
            pe.wait_ge(m_scaled, MB)
            for k in range(DT):
                for b in range(MB):
                    last = pe.transpose(ps[:, k // 4, (k % 4) * MEM + b * P:(k % 4) * MEM + (b + 1) * P],
                                        m_nat[:, b, k * P:(k + 1) * P], ident)
                if k % 4 == 3:
                    last.then_inc(m_turned, 1)
            pe.wait_ge(mT_done, DT)
            projections(0, PR_SB, lambda k: mT_hi[:, k, :], lambda k: mT_lo[:, k, :],
                        there=lambda k: pe.wait_ge(mT_split, k + 1))
            pe.wait_ge(pr_copied, 4)
            pe.wait_ge(pr_final, 4)
            for b in range(8):
                pe.wait_ge(x_in[b], 16)
                if b >= 2:
                    pe.wait_ge(xT_done, b - 1)
                for k in range(DT):
                    last = pe.transpose(ps[:, b % 2, k * P:(k + 1) * P], x_nat[:, b, k * P:(k + 1) * P], ident)
                last.then_inc(x_turned, 1)
            norm_sum(0)
            ffn(0, U_FFN1, 0)
            norm_sum(1)

            def sb_scores(s):
                head, j = s // 8, 7 - s % 8
                r, buf = (head % 2) * HD, (head // 2) % 2
                after(pe, sb_a_ready, s - 1)
                for c, d in bank_pieces(j * P, S):
                    last = mm(ps[:, s % 2, c:d], sb_k[r:r + HD, buf, j * P:(j + 1) * P], sb_q[r:r + HD, buf, c:d], True, False)
                last.then_inc(sb_z, 1)

            def sb_cumulate(s):
                j = 7 - s % 8
                pe.wait_ge(sb_sp_ready, s + 1)
                if j < 7:
                    pe.wait_ge(sb_sum_ready, sum_count(s - 1))
                for c, d in bank_pieces(j * P, S):
                    mm(ps[:, s % 2, c:d], neg_tri, sb_sp[:, s % 2, c:d], False, False)
                for c, d in bank_pieces((j + 1) * P, S):
                    mm(ps[:, s % 2, c:d], neg_ones, sb_sum[:, s % 2, c:d], False, False)
                mm(ps[:, s % 2, j * P:(j + 1) * P], ident, neg_mask, False, True).then_inc(sb_cum, 1)

            def sb_values(s):
                head, j = s // 8, 7 - s % 8
                r, buf = (head % 2) * HD, (head // 2) % 2
                pe.wait_ge(sb_a_ready, s + 1)
                if j == 7:
                    after(pe, sb_o, head)
                for c, d in bank_pieces(j * P, S):
                    last = mm(ps[r:r + HD, 2, c:d], sb_v[:, buf, j, r:r + HD], sb_a[:, s % 2, c:d], j == 7 or (j == 3 and c < 512), j == 0)
                last.then_inc(sb_av, 1)

            projections(PR_SB, PR_BESIDE, hh, hl, lambda k: pe.wait_ge(h_ready, 8 + k + 1))
            pe.wait_ge(pr_copied, PR_BESIDE)
            pe.wait_ge(pr_final, aux_before(PR_BESIDE))
            for pair in range(3):
                beside = beside_sb(pair)
                s0 = 16 * pair
                sb_scores(s0)
                for s in range(16):
                    f, phase = divmod(s, SB_EVERY)
                    products = f < len(beside) and phase < SB_EVERY - 1
                    if products:
                        proj(beside[f], hh, hl, k0=2 * phase, k1=2 * phase + 1)
                    if s + 1 < 16:
                        sb_scores(s0 + s + 1)
                    if products:
                        proj(beside[f], hh, hl, k0=2 * phase + 1, k1=2 * phase + 2)
                    elif f < len(beside):
                        proj_aux(beside[f])
                    if s:
                        sb_values(s0 + s - 1)
                    sb_cumulate(s0 + s)
                sb_values(s0 + 15)
                if pair < 2:
                    pe.wait_ge(pr_copied, beside[-1] + 1)
                    pe.wait_ge(pr_final, aux_before(beside[-1] + 1))

            def x_scores(n):
                h, half = divmod(n, 2)
                r = (h % 2) * HD
                after(pe, xa_sub, n)
                for b in range(4):
                    q0 = (4 * half + b) * P
                    last = mm(ps[:, 0, b * MEM:(b + 1) * MEM], x_q[r:r + HD, h // 2, q0:q0 + P], mkT[r:r + HD, h // 2, :], True, True)
                last.then_inc(xa_z, 1)

            def x_turn(n):
                pe.wait_ge(xa_prob, n + 1)
                after(pe, xa_pT, 2 * n)
                after(pe, xa_o, n)
                for mb in range(MB):
                    for b in range(4):
                        last = pe.transpose(ps[:, 1, mb * 512 + b * P:mb * 512 + (b + 1) * P], x_p[:, b, mb * P:(mb + 1) * P], ident)
                    last.then_inc(xa_turned, 1)

            def x_values(n):
                h = n // 2
                r = (h % 2) * HD
                for mb in range(MB):
                    pe.wait_ge(xa_pT, 2 * n + mb + 1)
                    last = mm(bank(2)[r:r + HD, :], mv[:, mb, h * HD:(h + 1) * HD], x_pT[:, mb, :], mb == 0, mb == MB - 1)
                last.then_inc(xa_pv, 1)

            pe.wait_ge(sb_o, 6)
            pe.wait_ge(pr_final, aux_before(PR_DIL))
            x_scores(0)
            for n in range(9):
                proj(PR_DIL + n, hh, hl, k1=DT // 2)
                if n < 8:
                    x_turn(n)
                if n + 1 < 8:
                    x_scores(n + 1)
                if n:
                    proj_aux(PR_DIL + n - 1)
                proj(PR_DIL + n, hh, hl, k0=DT // 2)
                if n < 8:
                    x_values(n)
            proj_aux(PR_DIL + 8)

            def d_scores(n):
                head, b = divmod(n, 8)
                r = head * HD
                after(pe, d_biased, n)
                q = lambda g: d_qk[r:r + HD, g, b * P:(b + 1) * P]
                kk = lambda g, c, d: d_qk[r:r + HD, 3 + g, c:d]
                a = (7 - b) * P
                for c, d in bank_pieces(a, 1024):
                    mm(ps_flat(c, d), q(2), kk(2, c - a, d - a), True, True)
                lo = max(b - 1, 0)
                mm(ps_flat(G0_AT + (lo - b + 1) * P, G0_AT + 2 * P), q(0), kk(0, lo * P, (b + 1) * P), True, True)
                for i in range(min(b, 4) + 1):
                    last = mm(ps_flat(G1_AT + i * P, G1_AT + (i + 1) * P), q(1), kk(1, (b - i) * P, (b - i + 1) * P), True, True)
                last.then_inc(d_z, 1)

            def d_turn(c):
                n, blocks, _, _ = chunks[c]
                pe.wait_ge(d_prob, n + 1)
                after(pe, d_pT_ready, c - 2)
                for i, (at_, _, _) in enumerate(blocks):
                    last = pe.transpose(bank(4 + c % 3)[:, i * P:(i + 1) * P], d_p[:, n % 2, at_:at_ + P], ident)
                last.then_inc(d_turned, 1)

            def d_values(c):
                n, blocks, begin, end = chunks[c]
                r = (n // 8) * HD
                pe.wait_ge(d_pT_ready, c + 1)
                if begin and n % 4 == 0:
                    after(pe, d_o, n // 4)
                for i, (_, g, kb) in enumerate(blocks):
                    last = mm(bank(7)[r:r + HD, (n % 4) * P:(n % 4 + 1) * P], v_dil(g)[:, kb, r:r + HD],
                              d_pT[:, c % 3, i * P:(i + 1) * P], begin and i == 0, end and i == len(blocks) - 1)
                last.then_inc(d_pv, 1)

            pe.wait_ge(xa_o, 8)
            pe.wait_ge(pr_final, aux_before(len(PROJ)))
            d_scores(0)
            for c in range(len(chunks) + 2):
                if c < len(chunks):
                    if chunks[c][2] and chunks[c][0] + 1 < 16:
                        d_scores(chunks[c][0] + 1)
                    d_turn(c)
                if c >= 2:
                    d_values(c - 2)

            pe.wait_ge(d_o, 4)
            for m in range(DT):
                u = U_MERGE + 4 * m
                for b in range(3):
                    pe.wait_ge(split_done, u + b + 1)
                    if m and b < 2:
                        pe.wait_ge(gated, 3 * (m - 1) + b + 2)
                    if m and b == 2:
                        pe.wait_ge(gate_done, 3 * m)
                    product(b, (u + b) % NW, hh, hl, S).then_inc(unit_done, 1)
                pe.wait_ge(split_done, u + 4)
                if m == 0:
                    pe.wait_ge(o_split, BR)
                for b in range(3):
                    if b == 0:
                        after(pe, gated, 3 * (m - 1) + 1)
                    else:
                        pe.wait_ge(gate_done, 3 * m + b)
                    k0, k1 = BR_OF[b]
                    product((3, 0, 1)[b], (u + 3) % NW, lambda k: oM_hi[:, k0 + k, :], lambda k: oM_lo[:, k0 + k, :], S,
                            tiles=k1 - k0, w0=k0).then_inc(br_done if b < 2 else unit_done, 1)

            for m in range(DT):
                u = U_OUT + m
                pe.wait_ge(split_done, u + 1)
                if m >= 2:
                    pe.wait_ge(x_added, m - 1)
                product(2 + m % 2, u % NW, hh, hl, S, there=(lambda k: pe.wait_ge(mg_split, k + 1)) if m == 0 else None
                        ).then_inc(unit_done, 1)
            norm_sum(2)
            ffn(1, U_FFN2, 2)

            pe.wait_ge(down_added, 16 * NGRP)
            for b in range(8):
                after(pe, y_ready[b % 2], b // 2)
                for k in range(DT):
                    last = pe.transpose(ps[:, b % 2, k * P:(k + 1) * P], xT[:, k, b * P:(b + 1) * P], ident)
                last.then_inc(y_turned, 1)


def dilated_plan(b):
    g2 = [((7 - b + k) * P, 2, k) for k in range(b + 1)]
    g0 = [(G0_AT + (k - b + 1) * P, 0, k) for k in range(max(b - 1, 0), b + 1)]
    g1 = [(G1_AT + i * P, 1, b - i) for i in range(min(b, 4) + 1)]
    end = G1_AT + (min(b, 4) + 1) * P
    segs = [((7 - b) * P, end)] if b else [(7 * P, 8 * P), (9 * P, end)]
    return segs, g2 + g0 + g1


def dilated_windows():
    back = TOE - 1 - P
    return ([(2, G2_AT, 8 * P, back - 7 * P), (0, G0_AT, 2 * P, back - P)]
            + [(1, G1_AT + i * P, P, back - i * P) for i in range(5)])


def t5_bucket(dist):
    exact, last, farthest = 16, 31, 2048
    if dist < exact:
        return dist
    f = np.float32
    large = exact + int(f(np.log(f(dist) / f(exact))) / f(np.log(farthest / exact)) * f(exact))
    return min(large, last)


def bias_onehot():
    t = np.zeros((33, NG, TOE), np.float32)
    for g, (w, d) in enumerate(DIL):
        for x in range(TOE):
            dist = S - 1 - x
            ok = 0 <= dist <= w and dist % d == 0
            t[t5_bucket(dist) if ok else 32, g, x] = 1.0
    return t.reshape(33, NG * TOE)


def constants():
    i, j = np.arange(P)[:, None], np.arange(P)[None, :]
    one = np.ones((P, P))
    tiles = [i == j, -1.0 * (i >= j), -one, one, i // HD == j // HD, i < j, NEG * (i >= j)]
    return np.ascontiguousarray(np.stack([np.asarray(t, np.float32) for t in tiles], axis=1))


def column_units(w, tiles):
    n = w.shape[0] // P
    return [w[:, c * P:(c + 1) * P].reshape(n, P, P).transpose(1, 0, 2).reshape(P, n * P) for c in tiles]


def swiglu_units(w_gu, w_down):
    def gu(g):
        return column_units(w_gu, [c for t in range(GT * g, GT * g + GT) for c in (t, FT + t)])

    def down(g):
        return [w_down[f * P:(f + 1) * P] for f in range(GT * g, GT * g + GT)]

    units = gu(0)
    for g in range(1, NGRP):
        units += gu(g) + down(g - 1)
    return units + down(NGRP - 1)


def weight_units(w_mem_kv, f1_gu, f1_down, w_in, w_br, w_out, f2_gu, f2_down):
    units = column_units(w_mem_kv, range(4)) + swiglu_units(f1_gu, f1_down)
    units += column_units(w_in, [q + 3 * i for q in range(3) for i in range(3)])
    units += column_units(w_in, [18, 19] + list(range(9, 18)))
    for m in range(DT):
        units += column_units(w_in, [20 + b * DT + m for b in range(3)])
        units += [np.pad(column_units(w_br, [m])[0], ((0, 0), (0, (DT - BR) * P)))]
    units += column_units(w_out, range(DT)) + swiglu_units(f2_gu, f2_down)
    return np.ascontiguousarray(np.stack(units))


_ORDER = ["x", "mem", "weights", "gains", "head_gains", "rel_bias", "consts", "onehot"]


def kernel(**inputs):
    import concourse.bacc as _bacc
    from concourse.bass_utils import run_bass_kernel_spmd as _run

    a = {k: np.asarray(v) for k, v in inputs.items()}
    w_br = np.concatenate([a["w_br_sb"][0], a["w_br_dil"][0], a["w_br_x"][0]], axis=0)
    arrays = {
        "x": a["x"][0],
        "mem": a["mem"][0],
        "weights": weight_units(a["w_mem_kv"][0], a["ffn1_w_gu"][0], a["ffn1_w_down"][0], a["w_in"][0], w_br,
                                a["w_out"][0], a["ffn2_w_gu"][0], a["ffn2_w_down"][0]),
        "gains": np.stack([a[n][0].reshape(DT, P).T for n in ("ffn1_norm", "mix_norm", "ffn2_norm", "mem_norm")], axis=1),
        "head_gains": np.stack([np.tile(a[n][0], 2) for n in ("dil_q_gain", "dil_k_gain", "x_q_gain", "x_k_gain")], axis=1),
        "rel_bias": a["rel_bias"],
        "consts": constants(),
        "onehot": bias_onehot(),
    }
    nc = _bacc.Bacc("TRN2", target_bir_lowering=False, num_devices=1)
    arrays = {f"in_{n}": np.ascontiguousarray(v) for n, v in arrays.items()}
    args = [nc.dram_tensor(f"in_{n}", arrays[f"in_{n}"].shape, F32, kind="ExternalInput").ap() for n in _ORDER]
    out = nc.dram_tensor("out_0", (S, D), F32, kind="ExternalOutput").ap()
    layer(nc, *args, out)
    r = _run(nc, [arrays], core_ids=[0])
    return r.results[0]["out_0"].reshape(1, S, D)
```

```python
from contextlib import ExitStack

import numpy as np
import concourse.bass as bass
from concourse import mybir

P = 128
D = 1024
S = 1024
DT = D // P
FF = 2816
FT = FF // P
MEM = 256
MB = MEM // P
HD = 64
HS, HDL, HX = 6, 6, 4
NG = 3
EPS = 1e-6
NEG = -1e30
GT = 2
NGRP = FT // GT
NRAW, NW = 2, 3
AHEAD = 2
BODY = 6 * GT

U_MEM = 0
U_FFN1 = U_MEM + 4
FFN_UNITS = 3 * FT
U_SB = U_FFN1 + FFN_UNITS
U_QX = U_SB + 9
U_DIL = U_QX + 2
U_MERGE = U_DIL + 9
U_OUT = U_MERGE + 4 * DT
U_FFN2 = U_OUT + DT
UNITS = U_FFN2 + FFN_UNITS
BR = (HS * HD + 2 * HD + HX * HD) // P
BR_OF = ((0, 3), (3, 4), (4, 6))

STRIP = 15 * P
G2_AT, G0_AT, G1_AT = 0, 8 * P, 10 * P
DIL = ((128, 1), (512, 4), (2048, 16))
TOE = 1152

F32 = mybir.dt.float32
F32R = mybir.dt.float32r
ALU = mybir.AluOpType
ACT = mybir.ActivationFunctionType
AX = mybir.AxisListType

PROJ = [("norm", MEM), ("norm", MEM), ("turn", MEM), ("turn", MEM)]
PROJ += [("copy", S), ("copy", S), ("turn", S)] * 3
PROJ += [("norm", S)] * 2 + [("norm", S)] * 6 + [("turn", S)] * 3
PR_SB, PR_QX, PR_DIL = 4, 13, 15
PR_BESIDE = PR_SB + 3


def count_before(kinds, n):
    return sum(k in kinds for k, _ in PROJ[:n])


def aux_before(n):
    return count_before(("norm", "turn"), n)


def proj_unit(n):
    return U_MEM + n if n < PR_SB else U_SB + n - PR_SB


def proj_pair(n):
    return 2 if n < PR_SB else n % 2 if n < PR_BESIDE else 3 if n < PR_DIL else 2 + (n - PR_DIL) % 2


def aux_pair(n):
    return proj_pair(n) if n >= PR_BESIDE else 3 if n < PR_SB else 2


def beside_sb(pair):
    return range(PR_BESIDE + 3 * pair, min(PR_BESIDE + 3 * pair + 3, PR_DIL))


TOE_PAIR = (2, 3, 0, 1)
SB_EVERY = 5


def bank_pieces(lo, hi):
    return [(a, b) for a, b in ((lo, min(hi, 512)), (max(lo, 512), hi)) if a < b]


def layer(nc, x, mem, weights, gains, head_gains, rel_bias, consts, onehot, out):
    ctx = ExitStack()
    with ctx:
        base = -(-nc.sbuf_base // 64) * 64

        def at(name, off, shape, dt=F32):
            return nc.alloc_sbuf_tensor_at(name, shape, dt, offset=base + off)

        def sem(name):
            return ctx.enter_context(nc.semaphore(name))

        K = 1024
        XT = 0
        HH, HL = 32 * K, 64 * K
        RAW = 96 * K
        WH, WL = RAW + 4 * K * NRAW, RAW + 4 * K * (NRAW + NW)
        MISC = WL + 4 * K * NW
        AR = MISC + 7936

        xT = at("xT", XT, [P, DT, S])
        h_hi = at("h_hi", HH, [P, DT, S], F32R)
        h_lo = at("h_lo", HL, [P, DT, S], F32R)
        raw = at("raw", RAW, [P, NRAW, 1024])
        w_hi = at("w_hi", WH, [P, NW, 8, P], F32R)
        w_lo = at("w_lo", WL, [P, NW, 8, P], F32R)
        cst = at("cst", MISC, [P, 7, P])
        ident, neg_tri, neg_ones, ones, head_ones, causal, neg_mask = (cst[:, i, :] for i in range(7))
        mkT = at("mkT", MISC + 3584, [P, 2, MEM])
        mv = at("mv", MISC + 3584 + 2048, [P, MB, MEM])
        sm = MISC + 3584 + 4096
        g32 = at("g32", sm, [P, 4, DT])
        small = at("small", sm + 128, [P, 26])
        hg, m_ss, m_rs, x_max, x_den, x_rden = (small[:, i:i + w] for i, w in ((0, 4), (4, MB), (6, MB), (8, 4), (12, 4), (16, 4)))
        eps_d, eps_h, b_max, b_nmax, b_den, b_rden = (small[:, i:i + 1] for i in range(20, 26))

        x_nat = at("x_nat", HH, [P, DT, 8, P])
        g_raw = at("g_raw", AR + 50 * K, [P, 4, DT])
        hg_raw = at("hg_raw", AR + 50 * K + 128, [P, 4])
        m_nat = at("m_nat", HL, [P, MB, D])
        m_sq = at("m_sq", HL + 8 * K, [P, D])
        mT = at("mT", HL + 12 * K, [P, DT, MEM])
        oh = at("oh", AR + 32 * K, [33, NG * TOE])
        mT_hi = at("mT_hi", AR, [P, DT, MEM], F32R)
        mT_lo = at("mT_lo", AR + 8 * K, [P, DT, MEM], F32R)
        rel = at("rel", AR + 16 * K, [33, 6])
        toe = at("toe", AR + 17 * K, [2, NG * TOE])

        a_hi = at("a_hi", AR, [P, 2 * GT, S], F32R)
        a_lo = at("a_lo", AR + 16 * K, [P, 2 * GT, S], F32R)
        silu = at("silu", AR + 32 * K, [P, 2, S])
        glu = at("glu", AR + 40 * K, [P, 2, S])
        sq = at("sq", AR + 56 * K, [P, 2, S])
        acc = at("acc", AR + 64 * K, [P, S])
        rB = at("rB", AR + 68 * K, [P, S])

        pr_mem = [at(f"pr_mem{i}", AR + (46 + i) * K, [P, MEM]) for i in range(3)]
        pr_x = [at(f"pr_x{i}", AR + (56 + 4 * i) * K, [P, S]) for i in range(3)]

        o_sb = at("o_sb", AR, [P, 3, S])
        o_dil = at("o_dil", AR + 12 * K, [P, S])
        o_x = at("o_x", AR + 16 * K, [P, 2, S])
        sb_q = at("sb_q", AR + 24 * K, [P, 2, S])
        sb_k = at("sb_k", AR + 32 * K, [P, 2, S])
        sb_v = at("sb_v", AR + 40 * K, [P, 2, 8, P])
        sb_l = at("sb_l", XT, [P, 2, S])
        sb_sp = at("sb_sp", XT + 8 * K, [P, 2, S])
        sb_sum = at("sb_sum", XT + 16 * K, [P, 2, S])
        sb_a = at("sb_a", XT + 24 * K, [P, 2, S])
        d_qk = at("d_qk", XT, [P, 6, S])
        d_v = at("d_v", XT + 24 * K, [P, 2, 8, P])
        d_v2 = at("d_v2", AR + 32 * K, [P, 8, P])
        bias = at("bias", AR + 36 * K, [P, 2, STRIP])
        d_p = at("d_p", AR + 52 * K, [P, 2, STRIP])
        d_pT = at("d_pT", AR + 24 * K, [P, 3, 512])
        x_q = at("x_q", AR + 48 * K, [P, 2, S])
        x_p = at("x_p", AR + 24 * K, [P, 4, MEM])
        x_pT = at("x_pT", AR + 28 * K, [P, MB, 512])
        oM_hi = at("oM_hi", XT, [P, BR, S], F32R)
        oM_lo = at("oM_lo", AR + 24 * K, [P, BR, S], F32R)
        gate = at("gate", AR + 48 * K, [P, 3, S])
        merged = at("merged", AR, [P, 6, S])
        merged2 = at("merged2", XT + 24 * K, [P, 2, S])
        x_back = at("x_back", AR + 24 * K, [P, DT, S])
        y_nat = at("y_nat", HH, [P, 8, D])

        ps = ctx.enter_context(nc.psum_tensor("ps", [P, 4, 1024], F32))

        x_keep = nc.dram_tensor("x_keep", (P, DT * S), F32, kind="Internal").ap()
        toe_keep = nc.dram_tensor("toe_keep", (2, P, NG * TOE), F32, kind="Internal").ap()

        x_in = [sem(f"x_in{i}") for i in range(8)]
        mem_in, cst_in, gain_in, hgain_in = sem("mem_in"), sem("cst_in"), sem("gain_in"), sem("hgain_in")
        onehot_in, rel_in = sem("onehot_in"), sem("rel_in")
        consts_ready = sem("consts_ready")
        gains_ready = sem("gains_ready")
        raw_in = [sem(f"raw_in{i}") for i in range(NRAW)]
        hi_done, split_done, unit_done = sem("hi_done"), sem("split_done"), sem("unit_done")
        toe_done, toe_kept, toe_out, bias_in = sem("toe_done"), sem("toe_kept"), sem("toe_out"), [sem("bias_in0"), sem("bias_in1")]
        m_ss_done, m_rs_done, m_scaled = sem("m_ss_done"), sem("m_rs_done"), sem("m_scaled")
        m_turned, mT_done, mT_hi_done, mT_split = sem("m_turned"), sem("mT_done"), sem("mT_hi_done"), sem("mT_split")
        x_turned, xT_done = sem("x_turned"), sem("xT_done")
        sq_done, acc_done, ss_done = sem("sq_done"), sem("acc_done"), sem("ss_done")
        ln_done, rstd_done, newton = sem("ln_done"), sem("rstd_done"), sem("newton")
        h_hi_done, h_ready = sem("h_hi_done"), sem("h_ready")
        gate_scaled, up_scaled, silu_done = sem("gate_scaled"), sem("up_scaled"), sem("silu_done")
        glu_done, a_hi_done, a_ready = sem("glu_done"), sem("a_hi_done"), sem("a_ready")
        down_done, down_added = sem("down_done"), sem("down_added")
        pr_copied, pr_sq_done = sem("pr_copied"), sem("pr_sq_done")
        pr_aux, pr_ln, pr_rstd, pr_newton, pr_final = (sem(f"pr_{n}") for n in ("aux", "ln", "rstd", "newton", "final"))
        x_kept, x_back_in = sem("x_kept"), sem("x_back_in")
        sb_z, sb_abs, sb_exp, sb_ln = sem("sb_z"), sem("sb_abs"), sem("sb_exp"), sem("sb_ln")
        sb_soft, sb_sp_ready, sb_sum_ready = sem("sb_soft"), sem("sb_sp_ready"), sem("sb_sum_ready")
        sb_cum, sb_a_ready, sb_av, sb_o = sem("sb_cum"), sem("sb_a_ready"), sem("sb_av"), sem("sb_o")
        d_z, d_biased, d_negmax, d_exp, d_rden, d_prob = (sem(f"d_{n}") for n in ("z", "biased", "negmax", "exp", "rden", "prob"))
        d_turned, d_pT_ready, d_pv, d_o, d_gap = (sem(f"d_{n}") for n in ("turned", "pT_ready", "pv", "o", "gap"))
        xa_z, xa_max, xa_sub, xa_exp, xa_sum, xa_rden, xa_prob = (
            sem(f"xa_{n}") for n in ("z", "max", "sub", "exp", "sum", "rden", "prob"))
        xa_turned, xa_pT, xa_pv, xa_o = (sem(f"xa_{n}") for n in ("turned", "pT", "pv", "o"))
        o_hi_done, o_split = sem("o_hi_done"), sem("o_split")
        mg_scaled, gate_done, gated, gated_sum = sem("mg_scaled"), sem("gate_done"), sem("gated"), sem("gated_sum")
        br_done = sem("br_done")
        mg_hi_done, mg_split = sem("mg_hi_done"), sem("mg_split")
        x_added = sem("x_added")
        y_turned, y_ready, y_out = sem("y_turned"), sem("y_ready"), sem("y_out")

        def after(eng, s, value):
            if not isinstance(value, int) or value > 0:
                eng.wait_ge(s, value)

        def at_turn(k, i, step=BODY):
            return k if i is None else step * i + k

        def o_tile(i):
            return o_sb[:, i, :] if i < 3 else o_dil[:, :] if i == 3 else o_x[:, i - 4, :]

        def merged_tile(m):
            return merged[:, m, :] if m < 6 else merged2[:, m - 6, :]

        def v_dil(g):
            return d_v[:, g] if g < 2 else d_v2

        def proj_dest(n):
            if n < 2:
                return mkT[:, n, :]
            if n < 4:
                return mv[:, :, (n - 2) * P:(n - 1) * P]
            if n < PR_QX:
                h = (n - PR_SB) // 3 % 2
                return (sb_q[:, h, :], sb_k[:, h, :], sb_v[:, h])[(n - PR_SB) % 3]
            if n < PR_DIL:
                return x_q[:, n - PR_QX, :]
            if n < PR_DIL + 6:
                return d_qk[:, n - PR_DIL, :]
            return v_dil(n - PR_DIL - 6)[:, :, :]

        def proj_gain(n):
            return 3 if n < 2 else 2 if n < PR_DIL else 0 if n < PR_DIL + 3 else 1

        def sum_count(s):
            head, i = divmod(s, 8)
            return head * 13 + (1 + 2 * i if i < 7 else 13)

        def bank(i):
            return ps[:, i // 2, (i % 2) * 512:(i % 2) * 512 + 512]

        def ps_flat(lo, hi):
            return ps[:, 0:2, :].rearrange("p a b -> p (a b)")[:, lo:hi]

        chunks = []
        for n in range(16):
            blocks = dilated_plan(n % 8)[1]
            chunks += [(n, blocks[c:c + 4], c == 0, c + 4 >= len(blocks)) for c in range(0, len(blocks), 4)]

        def chunks_before(n):
            return sum(c[0] < n for c in chunks)

        block = ctx.enter_context(nc.Block())

        @block.sync
        def _(sp):
            sp.dma_start(m_nat[:], mem.rearrange("(b p) d -> p b d", p=P)).then_inc(mem_in, 16)
            sp.dma_start(cst[:], consts).then_inc(cst_in, 16)
            sp.dma_start(oh[:], onehot).then_inc(onehot_in, 16)
            sp.dma_start(rel[0:32, :], rel_bias).then_inc(rel_in, 16)
            sp.dma_start(hg_raw[:], head_gains).then_inc(hgain_in, 16)
            sp.dma_start(g_raw[:], gains).then_inc(gain_in, 16)
            for r in range(NRAW):
                sp.dma_start(raw[:, r, :], weights[r]).then_inc(raw_in[r], 16)
            for k in range(DT):
                sp.dma_start(x_nat[:, k], x[:, k * P:(k + 1) * P].rearrange("(b p) c -> p b c", p=P)).then_inc(x_in[k], 16)
            with sp.Fori(1, UNITS // NRAW) as i:
                for r in range(NRAW):
                    sp.wait_ge(split_done, NRAW * i + r - NRAW + 1)
                    sp.dma_start(raw[:, r, :], weights[bass.ds(NRAW * i + r, 1)].rearrange("a p n -> p (a n)")
                                 ).then_inc(raw_in[r], 16)
            for m in range(DT):
                sp.wait_ge(y_ready, m + 1)
                sp.dma_start(out[:, m * P:(m + 1) * P].rearrange("(b p) c -> p b c", p=P),
                             y_nat[:, :, m * P:(m + 1) * P]).then_inc(y_out, 16)
            sp.wait_ge(y_out, 16 * DT)

        @block.gpsimd
        def _(pool):
            def square_sums(r):
                for k in range(1, DT):
                    pool.wait_ge(sq_done, DT * r + k + 1)
                    if k > 1:
                        pool.wait_ge(acc_done, (DT - 1) * r + k - 1)
                    nc.gpsimd.tensor_tensor(acc[:], acc[:], sq[:, k % 2, :], ALU.add).then_inc(acc_done, 1)

            square_sums(0)
            square_sums(1)
            for s in range(48):
                j = 7 - s % 8
                pool.wait_ge(sb_sp_ready, s + 1)
                if j == 0:
                    continue
                if s:
                    pool.wait_ge(sb_cum, s)
                    pool.wait_ge(sb_sum_ready, sum_count(s - 1))
                a, b = j * P, (j + 1) * P
                nc.gpsimd.tensor_copy(sb_sum[:, (s + 1) % 2, a:b], sb_sp[:, s % 2, a:b]).then_inc(sb_sum_ready, 1)
                if j < 7:
                    nc.gpsimd.tensor_tensor(sb_sum[:, (s + 1) % 2, b:], sb_sum[:, s % 2, b:], sb_sp[:, s % 2, b:],
                                            ALU.add).then_inc(sb_sum_ready, 1)
            square_sums(2)

        @block.scalar
        def _(act):
            def split_hi(k, i=None):
                if i is None and k >= UNITS:
                    return
                act.wait_ge(raw_in[k % NRAW], 16 * (at_turn(k // NRAW, i, BODY // NRAW) + 1))
                after(act, unit_done, at_turn(k, i) - NW + 1)
                nc.scalar.activation(w_hi[:, k % NW].rearrange("p a b -> p (a b)"), raw[:, k % NRAW, :],
                                     ACT.Copy).then_inc(hi_done, 1)

            def square(r, k):
                if k > 2:
                    act.wait_ge(acc_done, 7 * r + k - 2)
                nc.scalar.activation(sq[:, k % 2, :] if k else acc[:], xT[:, k, :], ACT.Square).then_inc(sq_done, 1)

            def gain_hi(k, gain):
                nc.scalar.activation(h_hi[:, k, :], xT[:, k, :], ACT.Copy, scale=g32[:, gain, k:k + 1]).then_inc(h_hi_done, 1)

            def rstd(r):
                act.wait_ge(ss_done, r + 1)
                nc.scalar.activation(rB[:], ps[:, 3, :], ACT.Ln, bias=eps_d[:, 0:1]).then_inc(ln_done, 1)
                act.wait_ge(ln_done, r + 1)
                nc.scalar.activation(rB[:], rB[:], ACT.Exp, scale=-0.5).then_inc(rstd_done, 1)
                act.wait_ge(rstd_done, 2 * r + 1)
                nc.scalar.activation(sq[:, 0, :], rB[:], ACT.Square).then_inc(rstd_done, 1)

            def ffn_tile(k, t, i=None):
                split_hi(k + AHEAD, i)
                act.wait_ge(gate_scaled, at_turn(t, i, 2 * GT) + 1)
                nc.scalar.activation(silu[:, t % 2, :], silu[:, t % 2, :], ACT.Silu).then_inc(silu_done, 1)
                split_hi(k + 1 + AHEAD, i)

            def ffn(f, u0):
                t0, u1 = FT * f, u0 + 2 * GT
                for q in range(GT):
                    ffn_tile(u0 + 2 * q, t0 + q)
                with act.Fori(0, (NGRP - 1) // 2) as i:
                    for half in range(2):
                        k = u1 + 3 * GT * half
                        for q in range(GT):
                            ffn_tile(k + 2 * q, t0 + GT * (1 + half) + q, i)
                        for q in range(GT):
                            split_hi(k + 2 * GT + q + AHEAD, i)
                for q in range(GT - 1):
                    split_hi(u0 + FFN_UNITS - GT + q + AHEAD)

            def proj_square(n):
                kind, w = PROJ[n]
                pr_sq, pr_rs, pr_vT = pr_mem if n < PR_SB else pr_x
                if kind == "norm":
                    act.wait_ge(pr_copied, n + 1)
                    after(act, pr_final, aux_before(n))
                    nc.scalar.activation(pr_sq[:, 0:w], proj_dest(n), ACT.Square).then_inc(pr_sq_done, 1)

            def proj_rstd(n):
                kind, w = PROJ[n]
                pr_sq, pr_rs, pr_vT = pr_mem if n < PR_SB else pr_x
                if kind == "norm":
                    i = count_before(("norm",), n)
                    act.wait_ge(pr_aux, aux_before(n) + 1)
                    nc.scalar.activation(pr_rs[:, 0:w], ps[:, aux_pair(n), 0:w], ACT.Ln, bias=eps_h[:, 0:1]).then_inc(pr_ln, 1)
                    act.wait_ge(pr_ln, i + 1)
                    nc.scalar.activation(pr_rs[:, 0:w], pr_rs[:, 0:w], ACT.Exp, scale=-0.5).then_inc(pr_rstd, 1)
                    act.wait_ge(pr_rstd, 2 * i + 1)
                    nc.scalar.activation(pr_sq[:, 0:w], pr_rs[:, 0:w], ACT.Square).then_inc(pr_rstd, 1)

            def projections(n0, n1):
                for n in range(n0, n1):
                    split_hi(proj_unit(n) + AHEAD)
                    if n > n0:
                        proj_rstd(n - 1)
                    proj_square(n)
                proj_rstd(n1 - 1)

            act.preload_act_table_set("natural_log_exp_and_others")
            act.wait_ge(mem_in, 16)
            for b in range(MB):
                if b:
                    act.wait_ge(m_ss_done, b)
                nc.scalar.activation(m_sq[:], m_nat[:, b, :], ACT.Square, accum_out=m_ss[:, b:b + 1]).then_inc(m_ss_done, 1)
            act.wait_ge(m_ss_done, MB)
            act.wait_ge(consts_ready, 2)
            nc.scalar.activation(m_rs[:], m_ss[:], ACT.Ln, bias=eps_d[:, 0:1]).then_inc(m_rs_done, 1)
            act.wait_ge(m_rs_done, 1)
            nc.scalar.activation(m_rs[:], m_rs[:], ACT.Exp, scale=-0.5).then_inc(m_rs_done, 1)
            split_hi(0)
            split_hi(1)
            for k in range(DT):
                act.wait_ge(mT_done, k + 1)
                nc.scalar.activation(mT_hi[:, k, :], mT[:, k, :], ACT.Copy).then_inc(mT_hi_done, 1)
            act.wait_ge(toe_kept, NG + 1)
            for hh in range(2):
                act.dma_start(toe_keep[hh:hh + 1, :, :], toe[hh:hh + 1, :].unsqueeze(1).to_broadcast([1, P, NG * TOE])
                              ).then_inc(toe_out, 16)
            for n in range(PR_SB):
                proj_square(n)
                split_hi(n + AHEAD)
                for k in (2 * n, 2 * n + 1):
                    act.wait_ge(xT_done, k + 1)
                    gain_hi(k, 0)
                proj_rstd(n)
                for k in (2 * n, 2 * n + 1):
                    square(0, k)
            rstd(0)
            ffn(0, U_FFN1)
            act.preload_act_table_set("natural_log_exp_and_others")
            for k in range(DT):
                act.wait_ge(down_added, DT * (NGRP - 1) + k + 1)
                gain_hi(k, 1)
                square(1, k)
            split_hi(U_FFN1 + FFN_UNITS - 1 + AHEAD)
            act.wait_ge(h_ready, 16)
            act.wait_ge(sq_done, 16)
            act.dma_start(x_keep[:, :], xT[:, :, :].rearrange("p k s -> p (k s)")).then_inc(x_kept, 16)
            rstd(1)

            def load_bias(hh):
                for g, c, w, x0 in dilated_windows():
                    src = bass.AP(toe_keep.tensor, (hh * P * NG + g) * TOE + x0, [[NG * TOE - 1, P], [1, w]])
                    act.dma_start(bias[:, hh, c:c + w], src).then_inc(bias_in[hh], 16)

            def d_evacuate(c):
                w = len(chunks[c][1]) * P
                act.wait_ge(d_turned, c + 1)
                after(act, d_pv, c - 2)
                nc.scalar.activation(d_pT[:, c % 3, 0:w], bank(4 + c % 3)[:, 0:w], ACT.Copy).then_inc(d_pT_ready, 1)

            def sb_explog(s):
                a = (7 - s % 8) * P
                act.wait_ge(sb_z, s + 1)
                after(act, sb_sp_ready, s - 1)
                nc.scalar.activation(sb_l[:, s % 2, a:], ps[:, s % 2, a:], ACT.Abs).then_inc(sb_abs, 1)
                act.wait_ge(sb_abs, s + 1)
                nc.scalar.activation(sb_l[:, s % 2, a:], sb_l[:, s % 2, a:], ACT.Exp, scale=-1.0).then_inc(sb_exp, 1)
                act.wait_ge(sb_exp, s + 1)
                nc.scalar.activation(sb_l[:, s % 2, a:], sb_l[:, s % 2, a:], ACT.Ln, bias=1.0).then_inc(sb_ln, 1)

            def sb_weights(s):
                a = (7 - s % 8) * P
                act.wait_ge(sb_cum, s + 1)
                after(act, sb_av, s - 1)
                nc.scalar.activation(sb_a[:, s % 2, a:], ps[:, s % 2, a:], ACT.Exp).then_inc(sb_a_ready, 1)

            projections(PR_SB, PR_BESIDE)
            act.wait_ge(x_kept, 16)
            for pair in range(3):
                beside = beside_sb(pair)
                for s in range(16):
                    f, phase = divmod(s, SB_EVERY)
                    if phase == 0:
                        if f:
                            if f <= len(beside):
                                proj_rstd(beside[f - 1])
                        if f < len(beside):
                            split_hi(proj_unit(beside[f]) + AHEAD)
                    sb_explog(16 * pair + s)
                    if s:
                        sb_weights(16 * pair + s - 1)
                    if phase == SB_EVERY - 1 and f < len(beside):
                        proj_square(beside[f])
                sb_weights(16 * pair + 15)

            act.wait_ge(sb_o, 6)
            act.wait_ge(toe_out, 32)
            load_bias(0)

            for n in range(10):
                p = PR_DIL + n
                if n < 8:
                    act.wait_ge(xa_sub, n + 1)
                    nc.scalar.activation(x_p[:], x_p[:], ACT.Exp).then_inc(xa_exp, 1)
                if n:
                    proj_square(p - 1)
                if n < 9:
                    split_hi(proj_unit(p) + AHEAD)
                if n < 8:
                    for b in range(MB):
                        act.wait_ge(xa_turned, 2 * n + b + 1)
                        after(act, xa_pv, n)
                        nc.scalar.activation(x_pT[:, b, :], ps[:, 1, 512 * b:512 * b + 512], ACT.Copy).then_inc(xa_pT, 1)
                if n:
                    proj_rstd(p - 1)
            act.wait_ge(xa_o, 8)
            load_bias(1)

            at_chunk = 0
            for n in range(16):
                segs, blocks = dilated_plan(n % 8)
                lo, hi = segs[0][0], segs[-1][1]
                act.wait_ge(d_negmax, n + 1)
                after(act, d_rden, n)
                nc.scalar.activation(d_p[:, n % 2, lo:hi], d_p[:, n % 2, lo:hi], ACT.Exp, bias=b_nmax[:, 0:1],
                                     accum_out=b_den[:, 0:1]).then_inc(d_exp, 1)
                for c in range(chunks_before(n - 1), chunks_before(n)) if n else ():
                    d_evacuate(c)
            for c in range(chunks_before(15), len(chunks)):
                d_evacuate(c)

            act.wait_ge(d_o, 4)
            for i in range(BR):
                nc.scalar.activation(oM_hi[:, i, :], o_tile(i), ACT.Copy).then_inc(o_hi_done, 1)
            for m in range(DT):
                u = U_MERGE + 4 * m
                for b in range(3):
                    split_hi(u + b + AHEAD)
                    act.wait_ge(mg_scaled, 3 * m + b + 1)
                    nc.scalar.activation(gate[:, b, :], gate[:, b, :], ACT.Sigmoid).then_inc(gate_done, 1)
                split_hi(u + 3 + AHEAD)

            act.wait_ge(unit_done, U_MERGE + 4 * DT - 1)
            for m in range(DT):
                act.wait_ge(gated_sum, 2 * m + 2)
                if m == DT - 1:
                    act.dma_start(x_back[:, :, :].rearrange("p k s -> p (k s)"), x_keep[:, :]).then_inc(x_back_in, 16)
                nc.scalar.activation(h_hi[:, m, :], merged_tile(m), ACT.Copy).then_inc(mg_hi_done, 1)
            act.preload_act_table_set("natural_log_exp_and_others")
            for m in range(DT):
                split_hi(U_OUT + m + AHEAD)
                if m < DT - 1:
                    act.wait_ge(x_added, m + 1)
                    square(2, m)
            act.wait_ge(unit_done, U_OUT + DT)
            for k in range(DT):
                if k == 3:
                    act.wait_ge(x_added, DT)
                    square(2, DT - 1)
                gain_hi(k, 2)
            rstd(2)
            ffn(1, U_FFN2)

            for m in range(DT):
                act.wait_ge(y_turned, m + 1)
                nc.scalar.activation(y_nat[:, :, m * P:(m + 1) * P], ps[:, m % 2, :].rearrange("p (b c) -> p b c", c=P),
                                     ACT.Copy).then_inc(y_ready, 1)

        def d_out(dve, n):
            hh, b = divmod(n, 8)
            dve.wait_ge(d_pv, chunks_before(n + 1))
            nc.vector.tensor_copy(o_dil[hh * HD:hh * HD + HD, (b - 3) * P:(b + 1) * P],
                                  bank(7)[hh * HD:hh * HD + HD, :]).then_inc(d_o, 1)

        @block.vector
        def _(dve):
            def split_lo(k, i=None):
                if i is None and k >= UNITS:
                    return
                dve.wait_ge(hi_done, at_turn(k, i) + 1)
                nc.vector.tensor_tensor(w_lo[:, k % NW].rearrange("p a b -> p (a b)"), raw[:, k % NRAW, :],
                                        w_hi[:, k % NW].rearrange("p a b -> p (a b)").bitcast(F32),
                                        ALU.subtract).then_inc(split_done, 1)

            def gain_lo(r, k, gain):
                dve.wait_ge(h_hi_done, DT * r + k + 1)
                nc.vector.scalar_tensor_tensor(out=h_lo[:, k, :], in0=xT[:, k, :], scalar=g32[:, gain, k:k + 1],
                                               in1=h_hi[:, k, :].bitcast(F32), op0=ALU.mult, op1=ALU.subtract
                                               ).then_inc(h_ready, 1)

            def newton_rstd(r):
                dve.wait_ge(rstd_done, 2 * r + 2)
                nc.vector.scalar_tensor_tensor(out=sq[:, 0, :], in0=ps[:, 3, :], scalar=D * EPS, in1=sq[:, 0, :],
                                               op0=ALU.add, op1=ALU.mult).then_inc(newton, 1)
                dve.wait_ge(newton, 3 * r + 1)
                nc.vector.tensor_scalar(sq[:, 0, :], sq[:, 0, :], -0.5, 1.5, ALU.mult, ALU.add).then_inc(newton, 1)
                dve.wait_ge(newton, 3 * r + 2)
                nc.vector.tensor_tensor(rB[:], rB[:], sq[:, 0, :], ALU.mult).then_inc(newton, 1)
                dve.wait_ge(newton, 3 * r + 3)

            def glu_tile(k, t, slot, i=None, between=None):
                split_lo(k - 1 + AHEAD, i)
                count = at_turn(t, i, 2 * GT)
                dve.wait_ge(unit_done, at_turn(k, i))
                after(dve, glu_done, count - 1)
                nc.vector.tensor_tensor(silu[:, t % 2, :], ps[:, 0, :], rB[:], ALU.mult).then_inc(gate_scaled, 1)
                split_lo(k + AHEAD, i)
                dve.wait_ge(unit_done, at_turn(k, i) + 1)
                after(dve, a_ready, count - 1)
                nc.vector.scalar_tensor_tensor(out=glu[:, t % 2, :], in0=ps[:, 1, :], scalar=0.5, in1=rB[:],
                                               op0=ALU.mult, op1=ALU.mult).then_inc(up_scaled, 1)
                dve.wait_ge(silu_done, count + 1)
                dve.wait_ge(up_scaled, count + 1)
                nc.vector.tensor_tensor(glu[:, t % 2, :], glu[:, t % 2, :], silu[:, t % 2, :], ALU.mult).then_inc(glu_done, 1)
                dve.wait_ge(glu_done, count + 1)
                nc.vector.tensor_copy(a_hi[:, slot, :], glu[:, t % 2, :]).then_inc(a_hi_done, 1)
                if between:
                    between()
                dve.wait_ge(a_hi_done, count + 1)
                nc.vector.tensor_tensor(a_lo[:, slot, :], glu[:, t % 2, :], a_hi[:, slot, :].bitcast(F32),
                                        ALU.subtract).then_inc(a_ready, 1)

            def add_tile(g, k, m, i=None):
                if m < DT - 1:
                    dve.wait_ge(down_done, at_turn((DT - 1) * g + m + 1, i, 2 * (DT - 1)))
                else:
                    dve.wait_ge(unit_done, at_turn(k + 1, i))
                nc.vector.tensor_tensor(xT[:, m, :], xT[:, m, :], ps[:, 2 + m % 2, :], ALU.add).then_inc(down_added, 1)

            def add_down(g, k, m0=0, i=None, finish=None):
                for m in range(m0, DT):
                    if m == 2:
                        split_lo(k - 1 + AHEAD, i)
                    add_tile(g, k, m, i)
                    if finish:
                        finish(m)
                split_lo(k + AHEAD, i)

            def ffn(f, u0, finish=None):
                t0, g0, u1 = FT * f, NGRP * f, u0 + 2 * GT
                for q in range(GT):
                    glu_tile(u0 + 2 * q + 1, t0 + q, q)
                with dve.Fori(0, (NGRP - 1) // 2) as i:
                    for half in range(2):
                        k = u1 + 3 * GT * half
                        g, last = g0 + half, k + 3 * GT - 1
                        for q in range(GT):
                            glu_tile(k + 2 * q + 1, t0 + GT * (1 + half) + q, GT * (1 - half) + q, i,
                                     (lambda: add_tile(g, last, 0, i)) if q == GT - 1 else None)
                        add_down(g, last, 1, i)
                add_down(g0 + NGRP - 1, u0 + FFN_UNITS - 1, finish=finish)

            def proj_copy(n):
                kind, w = PROJ[n]
                pr_sq, pr_rs, pr_vT = pr_mem if n < PR_SB else pr_x
                dve.wait_ge(unit_done, proj_unit(n) + 1)
                src = ps[:, proj_pair(n), 0:w]
                if kind == "turn":
                    after(dve, pr_aux, aux_before(n))
                to = pr_vT[:, 0:w] if kind == "turn" else proj_dest(n)
                if n < PR_SB:
                    nc.vector.tensor_copy(to, src).then_inc(pr_copied, 1)
                elif kind == "copy" and (n - PR_SB) % 3 == 0:
                    nc.vector.scalar_tensor_tensor(out=to, in0=src, scalar=HD ** -0.5, in1=rB[:],
                                                   op0=ALU.mult, op1=ALU.mult).then_inc(pr_copied, 1)
                else:
                    nc.vector.tensor_tensor(to, src, rB[:], ALU.mult).then_inc(pr_copied, 1)

            def proj_final(n):
                kind, w = PROJ[n]
                pr_sq, pr_rs, pr_vT = pr_mem if n < PR_SB else pr_x
                i, a = count_before(("norm",), n), aux_before(n)
                src = ps[:, aux_pair(n), 0:w]
                if kind == "norm":
                    dve.wait_ge(pr_rstd, 2 * i + 2)
                    nc.vector.scalar_tensor_tensor(out=pr_sq[:, 0:w], in0=src, scalar=HD * EPS, in1=pr_sq[:, 0:w],
                                                   op0=ALU.add, op1=ALU.mult).then_inc(pr_newton, 1)
                    c = proj_gain(n)
                    nc.vector.scalar_tensor_tensor(out=proj_dest(n), in0=proj_dest(n), scalar=hg[:, c:c + 1],
                                                   in1=pr_rs[:, 0:w], op0=ALU.mult, op1=ALU.mult).then_inc(pr_newton, 1)
                    dve.wait_ge(pr_newton, 3 * i + 2)
                    nc.vector.tensor_scalar(pr_sq[:, 0:w], pr_sq[:, 0:w], -0.5, 1.5, ALU.mult, ALU.add).then_inc(pr_newton, 1)
                    dve.wait_ge(pr_newton, 3 * i + 3)
                    nc.vector.tensor_tensor(proj_dest(n), proj_dest(n), pr_sq[:, 0:w], ALU.mult).then_inc(pr_final, 1)
                elif kind == "turn":
                    dve.wait_ge(pr_aux, a + 1)
                    nc.vector.tensor_copy(proj_dest(n), src.rearrange("p (b c) -> p b c", c=P)).then_inc(pr_final, 1)

            def projections(n0, n1):
                for n in range(n0, n1):
                    split_lo(proj_unit(n) + AHEAD)
                    if n > n0:
                        proj_final(n - 1)
                    proj_copy(n)
                proj_final(n1 - 1)

            nc.vector.memset(eps_d[:], D * EPS).then_inc(consts_ready, 1)
            nc.vector.memset(eps_h[:], HD * EPS).then_inc(consts_ready, 1)
            nc.vector.memset(rel[32:33, :], NEG).then_inc(consts_ready, 1)
            dve.wait_ge(gain_in, 16)
            nc.vector.tensor_scalar(g32[:], g_raw[:], float(D) ** 0.5, None, ALU.mult).then_inc(gains_ready, 1)
            dve.wait_ge(hgain_in, 16)
            nc.vector.tensor_scalar(hg[:, 0:1], hg_raw[:, 0:1], 1.0, None, ALU.mult).then_inc(gains_ready, 1)
            nc.vector.tensor_scalar(hg[:, 1:2], hg_raw[:, 1:2], 8.0, None, ALU.mult).then_inc(gains_ready, 1)
            nc.vector.tensor_scalar(hg[:, 2:3], hg_raw[:, 2:3], 1.0, None, ALU.mult).then_inc(gains_ready, 1)
            nc.vector.tensor_scalar(hg[:, 3:4], hg_raw[:, 3:4], 8.0, None, ALU.mult).then_inc(gains_ready, 1)
            dve.wait_ge(gains_ready, 5)
            dve.wait_ge(m_rs_done, 2)
            for b in range(MB):
                nc.vector.tensor_scalar(m_nat[:, b, :], m_nat[:, b, :], m_rs[:, b:b + 1], None, ALU.mult).then_inc(m_scaled, 1)
            for k in range(DT):
                dve.wait_ge(m_turned, k // 4 + 1)
                nc.vector.tensor_scalar(mT[:, k, :], ps[:, k // 4, (k % 4) * MEM:(k % 4 + 1) * MEM],
                                        g32[:, 3, k:k + 1], None, ALU.mult).then_inc(mT_done, 1)
            split_lo(0)
            split_lo(1)
            for k in range(DT):
                dve.wait_ge(mT_hi_done, k + 1)
                nc.vector.tensor_tensor(mT_lo[:, k, :], mT[:, k, :], mT_hi[:, k, :].bitcast(F32),
                                        ALU.subtract).then_inc(mT_split, 1)
            for q in range(NG):
                dve.wait_ge(toe_done, q + 1)
                nc.vector.tensor_copy(toe[:, q * TOE:q * TOE + 1024], ps[0:2, TOE_PAIR[q], :]).then_inc(toe_kept, 1)
            nc.vector.tensor_copy(toe[:, :].rearrange("p (g n) -> p g n", g=NG)[:, :, 1024:TOE],
                                  ps[0:2, TOE_PAIR[3], 0:NG * P].rearrange("p (g n) -> p g n", g=NG)).then_inc(toe_kept, 1)
            for n in range(PR_SB):
                proj_copy(n)
                for k in (2 * n, 2 * n + 1):
                    dve.wait_ge(x_turned, k + 1)
                    nc.vector.tensor_copy(xT[:, k, :], ps[:, k % 2, :]).then_inc(xT_done, 1)
                split_lo(n + AHEAD)
                for k in (2 * n, 2 * n + 1):
                    gain_lo(0, k, 0)
                proj_final(n)
            newton_rstd(0)
            dve.wait_ge(toe_out, 32)
            ffn(0, U_FFN1, lambda m: gain_lo(1, m - 1, 1) if m else None)
            gain_lo(1, DT - 1, 1)
            newton_rstd(1)

            def x_subtract(n):
                z = ps[:, 0, :].rearrange("p (b m) -> p b m", b=4)
                dve.wait_ge(xa_z, n + 1)
                after(dve, xa_prob, n)
                nc.vector.tensor_reduce(x_max[:], z, AX.X, ALU.max).then_inc(xa_max, 1)
                dve.wait_ge(xa_max, n + 1)
                after(dve, xa_turned, 2 * n)
                nc.vector.tensor_tensor(x_p[:], z, x_max[:].unsqueeze(2).to_broadcast([P, 4, MEM]),
                                        ALU.subtract).then_inc(xa_sub, 1)

            def x_divide(n):
                dve.wait_ge(xa_exp, n + 1)
                nc.vector.tensor_reduce(x_den[:], x_p[:], AX.X, ALU.add).then_inc(xa_sum, 1)
                dve.wait_ge(xa_sum, n + 1)
                nc.vector.reciprocal(x_rden[:], x_den[:]).then_inc(xa_rden, 1)
                dve.wait_ge(xa_rden, n + 1)
                nc.vector.tensor_tensor(x_p[:], x_p[:], x_rden[:].unsqueeze(2).to_broadcast([P, 4, MEM]),
                                        ALU.mult).then_inc(xa_prob, 1)

            def sb_softplus(s):
                a = (7 - s % 8) * P
                dve.wait_ge(sb_ln, s + 1)
                if s >= 2:
                    dve.wait_ge(sb_cum, s - 1)
                    dve.wait_ge(sb_sum_ready, sum_count(s - 2))
                nc.vector.scalar_tensor_tensor(out=sb_sp[:, s % 2, a:], in0=ps[:, s % 2, a:], scalar=0.0,
                                               in1=sb_l[:, s % 2, a:], op0=ALU.max, op1=ALU.add).then_inc(sb_soft, 1)
                dve.wait_ge(sb_soft, s + 1)
                nc.vector.tensor_tensor(sb_sp[:, s % 2, a:a + P], sb_sp[:, s % 2, a:a + P], causal,
                                        ALU.mult).then_inc(sb_sp_ready, 1)

            def sb_out(head):
                r = (head % 2) * HD
                dve.wait_ge(sb_av, 8 * head + 8)
                nc.vector.tensor_copy(o_sb[r:r + HD, head // 2, :], ps[r:r + HD, 2, :]).then_inc(sb_o, 1)

            projections(PR_SB, PR_BESIDE)
            dve.wait_ge(x_kept, 16)
            for pair in range(3):
                beside = beside_sb(pair)
                for s in range(16):
                    f, phase = divmod(s, SB_EVERY)
                    if phase == 0 and f < len(beside):
                        split_lo(proj_unit(beside[f]) + AHEAD)
                    sb_softplus(16 * pair + s)
                    if phase == 0 and 0 < f <= len(beside):
                        proj_final(beside[f - 1])
                    if phase == SB_EVERY - 1 and f < len(beside):
                        proj_copy(beside[f])
                    if s == 8:
                        sb_out(2 * pair)
                sb_out(2 * pair + 1)

            for n in range(10):
                p = PR_DIL + n
                if n < 8:
                    x_subtract(n)
                if n:
                    proj_copy(p - 1)
                if 0 < n < 9:
                    h, half = divmod(n - 1, 2)
                    r = (h % 2) * HD
                    dve.wait_ge(xa_pv, n)
                    nc.vector.tensor_copy(o_x[r:r + HD, h // 2, 512 * half:512 * half + 512],
                                          bank(2)[r:r + HD, :]).then_inc(xa_o, 1)
                if n < 8:
                    x_divide(n)
                if n < 9:
                    split_lo(proj_unit(p) + AHEAD)
                if n:
                    proj_final(p - 1)

            gap_done = 0
            for n in range(16):
                hh, b = divmod(n, 8)
                segs, blocks = dilated_plan(b)
                lo, hi = segs[0][0], segs[-1][1]
                if b == 0:
                    dve.wait_ge(bias_in[hh], 16 * 7)
                dve.wait_ge(d_z, n + 1)
                if n > 1:
                    dve.wait_ge(d_turned, chunks_before(n - 1))
                if n:
                    dve.wait_ge(d_exp, n)
                if len(segs) == 1:
                    nc.vector.tensor_tensor_reduce(d_p[:, n % 2, lo:hi], ps_flat(lo, hi), bias[:, hh, lo:hi], 1.0, -3e38,
                                                   ALU.add, ALU.max, b_max[:, 0:1]).then_inc(d_biased, 1)
                else:
                    for c, d in segs:
                        nc.vector.tensor_tensor(d_p[:, n % 2, c:d], ps_flat(c, d), bias[:, hh, c:d], ALU.add).then_inc(d_gap, 1)
                    nc.vector.memset(d_p[:, n % 2, segs[0][1]:segs[1][0]], NEG).then_inc(d_gap, 1)
                    gap_done += 3
                    dve.wait_ge(d_gap, gap_done)
                    nc.vector.tensor_reduce(b_max[:, 0:1], d_p[:, n % 2, lo:hi], AX.X, ALU.max).then_inc(d_biased, 1)
                dve.wait_ge(d_biased, n + 1)
                nc.vector.tensor_scalar(b_nmax[:], b_max[:], -1.0, None, ALU.mult).then_inc(d_negmax, 1)
                dve.wait_ge(d_exp, n + 1)
                after(dve, d_prob, n)
                nc.vector.reciprocal(b_rden[:], b_den[:]).then_inc(d_rden, 1)
                dve.wait_ge(d_rden, n + 1)
                nc.vector.tensor_scalar(d_p[:, n % 2, lo:hi], d_p[:, n % 2, lo:hi], b_rden[:, 0:1], None,
                                        ALU.mult).then_inc(d_prob, 1)
                if n % 4 == 1 and n > 1:
                    d_out(dve, n - 2)
            d_out(dve, 15)

            def merged_lo(m):
                dve.wait_ge(mg_hi_done, m + 1)
                nc.vector.tensor_tensor(h_lo[:, m, :], merged_tile(m), h_hi[:, m, :].bitcast(F32),
                                        ALU.subtract).then_inc(mg_split, 1)

            for i in range(BR):
                dve.wait_ge(o_hi_done, i + 1)
                nc.vector.tensor_tensor(oM_lo[:, i, :], o_tile(i), oM_hi[:, i, :].bitcast(F32),
                                        ALU.subtract).then_inc(o_split, 1)
            for m in range(DT):
                u = U_MERGE + 4 * m
                for b in range(3):
                    split_lo(u + b + AHEAD)
                    dve.wait_ge(unit_done, u + b + 1)
                    if b:
                        after(dve, gated_sum, 2 * (m - 1) + b)
                    else:
                        after(dve, gated, 3 * (m - 1) + 1)
                    nc.vector.tensor_tensor(gate[:, b, :], ps[:, b, :], rB[:], ALU.mult).then_inc(mg_scaled, 1)
                split_lo(u + 3 + AHEAD)
                if m == DT - 1:
                    for k in range(DT - 2):
                        merged_lo(k)
                for b in range(3):
                    pair = (3, 0, 1)[b]
                    dve.wait_ge(gate_done, 3 * m + b + 1)
                    if b < 2:
                        dve.wait_ge(br_done, 2 * m + b + 1)
                    else:
                        dve.wait_ge(unit_done, u + 4)
                    to = merged_tile(m) if b == 0 else gate[:, b, :]
                    nc.vector.tensor_tensor(to, gate[:, b, :], ps[:, pair, :], ALU.mult).then_inc(gated, 1)
                for b in range(1, 3):
                    dve.wait_ge(gated, 3 * m + 3)
                    if b == 2:
                        dve.wait_ge(gated_sum, 2 * m + 1)
                    nc.vector.tensor_tensor(merged_tile(m), merged_tile(m), gate[:, b, :], ALU.add).then_inc(gated_sum, 1)

            for m in (DT - 2, DT - 1):
                merged_lo(m)
            dve.wait_ge(x_back_in, 16)
            dve.wait_ge(mg_split, DT)
            for m in range(DT):
                split_lo(U_OUT + m + AHEAD)
                dve.wait_ge(unit_done, U_OUT + m + 1)
                nc.vector.tensor_tensor(xT[:, m, :], x_back[:, m, :], ps[:, 2 + m % 2, :], ALU.add).then_inc(x_added, 1)
            for k in range(DT):
                gain_lo(2, k, 2)
            newton_rstd(2)
            ffn(1, U_FFN2)

        @block.tensor
        def _(pe):
            def mm(o, a, b, start, stop):
                return pe.matmul(o, a, b, start=start, stop=stop, skip_group_check=True)

            def product(pair, slot, hi, lo, width, tiles=DT, w0=0, there=None, k0=0, k1=None):
                halves = [(c, min(c + 512, width)) for c in range(0, width, 512)]
                for k in range(k0, tiles if k1 is None else k1):
                    if there:
                        there(k)
                    first, final = k == 0, k == tiles - 1
                    for c, d in halves:
                        mm(ps[:, pair, c:d], w_hi[:, slot, w0 + k, :], hi(k)[:, c:d], first, False)
                        mm(ps[:, pair, c:d], w_hi[:, slot, w0 + k, :], lo(k)[:, c:d], False, False)
                    for c, d in halves:
                        last = mm(ps[:, pair, c:d], w_lo[:, slot, w0 + k, :], hi(k)[:, c:d], False, final)
                return last

            def hh(k):
                return h_hi[:, k, :]

            def hl(k):
                return h_lo[:, k, :]

            def gate_up(k, t, i=None, there=None, between=None):
                for part in range(2):
                    pe.wait_ge(split_done, at_turn(k, i) + part + 1)
                    after(pe, (gate_scaled, up_scaled)[part], at_turn(t, i, 2 * GT))
                    product(part, (k + part) % NW, hh, hl, S, there=there if part == 0 else None).then_inc(unit_done, 1)
                    if part == 0 and between:
                        between()

            def down(g, k, slot, i=None, finish=None):
                pe.wait_ge(split_done, at_turn(k, i) + GT)
                pe.wait_ge(a_ready, at_turn(GT * g, i, 2 * GT) + GT)
                for m in range(DT):
                    pair = 2 + m % 2
                    if m >= 2 or i is None:
                        pe.wait_ge(down_added, at_turn(DT * g, i, 2 * DT) + m - 1)
                    for q in range(GT):
                        s = (k + q) % NW
                        for c in (0, 512):
                            mm(ps[:, pair, c:c + 512], w_hi[:, s, m, :], a_hi[:, slot + q, c:c + 512], q == 0, False)
                            mm(ps[:, pair, c:c + 512], w_hi[:, s, m, :], a_lo[:, slot + q, c:c + 512], False, False)
                        for c in (0, 512):
                            last = mm(ps[:, pair, c:c + 512], w_lo[:, s, m, :], a_hi[:, slot + q, c:c + 512], False, q == GT - 1)
                    if m < DT - 1:
                        last.then_inc(down_done, 1)
                    else:
                        last.then_inc(unit_done, GT)
                    if finish:
                        finish(m)

            def ffn(f, u0, r, finish=None):
                t0, g0, u1 = FT * f, NGRP * f, u0 + 2 * GT
                gate_up(u0, t0, there=lambda k: pe.wait_ge(h_ready, 8 * r + k + 1), between=lambda: norm_sum(r))
                for q in range(1, GT):
                    gate_up(u0 + 2 * q, t0 + q)
                with pe.Fori(0, (NGRP - 1) // 2) as i:
                    for half in range(2):
                        k = u1 + 3 * GT * half
                        for q in range(GT):
                            gate_up(k + 2 * q, t0 + GT * (1 + half) + q, i)
                        down(g0 + half, k + 2 * GT, GT * half, i)
                down(g0 + NGRP - 1, u0 + FFN_UNITS - GT, 0, finish=finish)

            def norm_sum(r):
                pe.wait_ge(acc_done, 7 * r + 7)
                if r == 0:
                    pe.wait_ge(pr_final, PR_SB)
                elif r == 1:
                    pe.wait_ge(down_added, DT * NGRP)
                else:
                    pe.wait_ge(x_added, DT)
                for c in (0, 512):
                    last = mm(ps[:, 3, c:c + 512], ones, acc[:, c:c + 512], True, True)
                last.then_inc(ss_done, 1)

            def proj(n, hi, lo, there=None, k0=0, k1=DT):
                kind, w = PROJ[n]
                if k0 == 0:
                    pe.wait_ge(split_done, proj_unit(n) + 1)
                    if n < PR_BESIDE:
                        after(pe, pr_copied, n if n < PR_SB else n - 1)
                    else:
                        before = n if n < PR_DIL else n - 1
                        pe.wait_ge(pr_copied, before)
                        pe.wait_ge(pr_final, aux_before(before))
                last = product(proj_pair(n), proj_unit(n) % NW, hi, lo, w, there=there, k0=k0, k1=k1)
                if k1 == DT:
                    last.then_inc(unit_done, 1)

            def proj_aux(n):
                kind, w = PROJ[n]
                pr_sq, pr_rs, pr_vT = pr_mem if n < PR_SB else pr_x
                i, a, to = count_before(("norm",), n), aux_before(n), aux_pair(n)
                if kind == "norm":
                    pe.wait_ge(pr_sq_done, i + 1)
                elif kind == "turn":
                    pe.wait_ge(pr_copied, n + 1)
                if kind != "copy":
                    after(pe, pr_final, a)
                if kind == "norm":
                    for c in range(0, w, 512):
                        d = min(w, c + 512)
                        last = mm(ps[:, to, c:d], head_ones, pr_sq[:, c:d], True, True)
                    last.then_inc(pr_aux, 1)
                elif kind == "turn":
                    for b in range(w // P):
                        last = pe.transpose(ps[:, to, b * P:(b + 1) * P], pr_vT[:, b * P:(b + 1) * P], ident)
                    last.then_inc(pr_aux, 1)

            def projections(n0, n1, hi, lo, there=None):
                for n in range(n0, n1):
                    proj(n, hi, lo, there if n == n0 else None)
                    if n == n0:
                        norm_sum(1)
                    else:
                        proj_aux(n - 1)
                proj_aux(n1 - 1)

            pe.wait_ge(cst_in, 16)
            pe.wait_ge(m_scaled, MB)
            for k in range(DT):
                for b in range(MB):
                    last = pe.transpose(ps[:, k // 4, (k % 4) * MEM + b * P:(k % 4) * MEM + (b + 1) * P],
                                        m_nat[:, b, k * P:(k + 1) * P], ident)
                if k % 4 == 3:
                    last.then_inc(m_turned, 1)
            pe.wait_ge(onehot_in, 16)
            pe.wait_ge(rel_in, 16)
            pe.wait_ge(consts_ready, 3)
            for g in range(NG):
                if g == 2:
                    pe.wait_ge(mT_done, DT)
                    for gg in range(NG):
                        mm(ps[0:2, TOE_PAIR[3], gg * P:(gg + 1) * P], rel[:, 2 * gg:2 * gg + 2],
                           oh[:, gg * TOE + 1024:(gg + 1) * TOE], True, True)
                for c in (0, 512):
                    last = mm(ps[0:2, TOE_PAIR[g], c:c + 512], rel[:, 2 * g:2 * g + 2],
                              oh[:, g * TOE + c:g * TOE + c + 512], True, True)
                last.then_inc(toe_done, 1)
            pe.wait_ge(toe_kept, NG + 1)
            for n in range(PR_SB):
                proj(n, lambda k: mT_hi[:, k, :], lambda k: mT_lo[:, k, :],
                     there=(lambda k: pe.wait_ge(mT_split, k + 1)) if n == 0 else None)
                for k in (2 * n, 2 * n + 1):
                    pe.wait_ge(x_in[k], 16)
                    if k >= 2:
                        pe.wait_ge(xT_done, k - 1)
                    for b in range(8):
                        last = pe.transpose(ps[:, k % 2, b * P:(b + 1) * P], x_nat[:, k, b, :], ident)
                    last.then_inc(x_turned, 1)
                proj_aux(n)
            pe.wait_ge(xT_done, DT)
            ffn(0, U_FFN1, 0)

            def sb_scores(s):
                head, j = s // 8, 7 - s % 8
                r, buf = (head % 2) * HD, (head // 2) % 2
                after(pe, sb_a_ready, s - 1)
                for c, d in bank_pieces(j * P, S):
                    last = mm(ps[:, s % 2, c:d], sb_k[r:r + HD, buf, j * P:(j + 1) * P], sb_q[r:r + HD, buf, c:d], True, False)
                last.then_inc(sb_z, 1)

            def sb_cumulate(s):
                j = 7 - s % 8
                pe.wait_ge(sb_sp_ready, s + 1)
                if j < 7:
                    pe.wait_ge(sb_sum_ready, sum_count(s - 1))
                for c, d in bank_pieces(j * P, S):
                    mm(ps[:, s % 2, c:d], neg_tri, sb_sp[:, s % 2, c:d], False, False)
                for c, d in bank_pieces((j + 1) * P, S):
                    mm(ps[:, s % 2, c:d], neg_ones, sb_sum[:, s % 2, c:d], False, False)
                mm(ps[:, s % 2, j * P:(j + 1) * P], ident, neg_mask, False, True).then_inc(sb_cum, 1)

            def sb_values(s):
                head, j = s // 8, 7 - s % 8
                r, buf = (head % 2) * HD, (head // 2) % 2
                pe.wait_ge(sb_a_ready, s + 1)
                if j == 7:
                    after(pe, sb_o, head)
                for c, d in bank_pieces(j * P, S):
                    last = mm(ps[r:r + HD, 2, c:d], sb_v[:, buf, j, r:r + HD], sb_a[:, s % 2, c:d], j == 7 or (j == 3 and c < 512), j == 0)
                last.then_inc(sb_av, 1)

            projections(PR_SB, PR_BESIDE, hh, hl, lambda k: pe.wait_ge(h_ready, 8 + k + 1))
            pe.wait_ge(pr_copied, PR_BESIDE)
            pe.wait_ge(pr_final, aux_before(PR_BESIDE))
            for pair in range(3):
                beside = beside_sb(pair)
                s0 = 16 * pair
                sb_scores(s0)
                for s in range(16):
                    f, phase = divmod(s, SB_EVERY)
                    products = f < len(beside) and phase < SB_EVERY - 1
                    if products:
                        proj(beside[f], hh, hl, k0=2 * phase, k1=2 * phase + 1)
                    if s + 1 < 16:
                        sb_scores(s0 + s + 1)
                    if products:
                        proj(beside[f], hh, hl, k0=2 * phase + 1, k1=2 * phase + 2)
                    elif f < len(beside):
                        proj_aux(beside[f])
                    if s:
                        sb_values(s0 + s - 1)
                    sb_cumulate(s0 + s)
                sb_values(s0 + 15)
                if pair < 2:
                    pe.wait_ge(pr_copied, beside[-1] + 1)
                    pe.wait_ge(pr_final, aux_before(beside[-1] + 1))

            def x_scores(n):
                h, half = divmod(n, 2)
                r = (h % 2) * HD
                after(pe, xa_sub, n)
                for b in range(4):
                    q0 = (4 * half + b) * P
                    last = mm(ps[:, 0, b * MEM:(b + 1) * MEM], x_q[r:r + HD, h // 2, q0:q0 + P], mkT[r:r + HD, h // 2, :], True, True)
                last.then_inc(xa_z, 1)

            def x_turn(n):
                pe.wait_ge(xa_prob, n + 1)
                after(pe, xa_pT, 2 * n)
                after(pe, xa_o, n)
                for mb in range(MB):
                    for b in range(4):
                        last = pe.transpose(ps[:, 1, mb * 512 + b * P:mb * 512 + (b + 1) * P], x_p[:, b, mb * P:(mb + 1) * P], ident)
                    last.then_inc(xa_turned, 1)

            def x_values(n):
                h = n // 2
                r = (h % 2) * HD
                for mb in range(MB):
                    pe.wait_ge(xa_pT, 2 * n + mb + 1)
                    last = mm(bank(2)[r:r + HD, :], mv[:, mb, h * HD:(h + 1) * HD], x_pT[:, mb, :], mb == 0, mb == MB - 1)
                last.then_inc(xa_pv, 1)

            pe.wait_ge(sb_o, 6)
            pe.wait_ge(pr_final, aux_before(PR_DIL))
            x_scores(0)
            for n in range(9):
                proj(PR_DIL + n, hh, hl, k1=DT // 2)
                if n < 8:
                    x_turn(n)
                if n + 1 < 8:
                    x_scores(n + 1)
                if n:
                    proj_aux(PR_DIL + n - 1)
                proj(PR_DIL + n, hh, hl, k0=DT // 2)
                if n < 8:
                    x_values(n)
            proj_aux(PR_DIL + 8)

            def d_scores(n):
                head, b = divmod(n, 8)
                r = head * HD
                after(pe, d_biased, n)
                q = lambda g: d_qk[r:r + HD, g, b * P:(b + 1) * P]
                kk = lambda g, c, d: d_qk[r:r + HD, 3 + g, c:d]
                a = (7 - b) * P
                for c, d in bank_pieces(a, 1024):
                    mm(ps_flat(c, d), q(2), kk(2, c - a, d - a), True, True)
                lo = max(b - 1, 0)
                mm(ps_flat(G0_AT + (lo - b + 1) * P, G0_AT + 2 * P), q(0), kk(0, lo * P, (b + 1) * P), True, True)
                for i in range(min(b, 4) + 1):
                    last = mm(ps_flat(G1_AT + i * P, G1_AT + (i + 1) * P), q(1), kk(1, (b - i) * P, (b - i + 1) * P), True, True)
                last.then_inc(d_z, 1)

            def d_turn(c):
                n, blocks, _, _ = chunks[c]
                pe.wait_ge(d_prob, n + 1)
                after(pe, d_pT_ready, c - 2)
                for i, (at_, _, _) in enumerate(blocks):
                    last = pe.transpose(bank(4 + c % 3)[:, i * P:(i + 1) * P], d_p[:, n % 2, at_:at_ + P], ident)
                last.then_inc(d_turned, 1)

            def d_values(c):
                n, blocks, begin, end = chunks[c]
                r = (n // 8) * HD
                pe.wait_ge(d_pT_ready, c + 1)
                if begin and n % 4 == 0:
                    after(pe, d_o, n // 4)
                for i, (_, g, kb) in enumerate(blocks):
                    last = mm(bank(7)[r:r + HD, (n % 4) * P:(n % 4 + 1) * P], v_dil(g)[:, kb, r:r + HD],
                              d_pT[:, c % 3, i * P:(i + 1) * P], begin and i == 0, end and i == len(blocks) - 1)
                last.then_inc(d_pv, 1)

            pe.wait_ge(xa_o, 8)
            pe.wait_ge(pr_final, aux_before(len(PROJ)))
            d_scores(0)
            for c in range(len(chunks) + 2):
                if c < len(chunks):
                    if chunks[c][2] and chunks[c][0] + 1 < 16:
                        d_scores(chunks[c][0] + 1)
                    d_turn(c)
                if c >= 2:
                    d_values(c - 2)

            pe.wait_ge(d_o, 4)
            for m in range(DT):
                u = U_MERGE + 4 * m
                for b in range(3):
                    pe.wait_ge(split_done, u + b + 1)
                    if m and b < 2:
                        pe.wait_ge(gated, 3 * (m - 1) + b + 2)
                    if m and b == 2:
                        pe.wait_ge(mg_scaled, 3 * m)
                    product(b, (u + b) % NW, hh, hl, S).then_inc(unit_done, 1)
                pe.wait_ge(split_done, u + 4)
                if m == 0:
                    pe.wait_ge(o_split, BR)
                for b in range(3):
                    if b == 0:
                        after(pe, gated, 3 * (m - 1) + 1)
                    else:
                        pe.wait_ge(mg_scaled, 3 * m + b)
                    k0, k1 = BR_OF[b]
                    product((3, 0, 1)[b], (u + 3) % NW, lambda k: oM_hi[:, k0 + k, :], lambda k: oM_lo[:, k0 + k, :], S,
                            tiles=k1 - k0, w0=k0).then_inc(br_done if b < 2 else unit_done, 1)

            for m in range(DT):
                u = U_OUT + m
                pe.wait_ge(split_done, u + 1)
                if m >= 2:
                    pe.wait_ge(x_added, m - 1)
                product(2 + m % 2, u % NW, hh, hl, S, there=(lambda k: pe.wait_ge(mg_split, k + 1)) if m == 0 else None
                        ).then_inc(unit_done, 1)
            def y_turn(m):
                if m >= 2:
                    pe.wait_ge(y_ready, m - 1)
                else:
                    pe.wait_ge(glu_done, 2 * FT)
                pe.wait_ge(down_added, DT * (2 * NGRP - 1) + m + 1)
                for b in range(8):
                    last = pe.transpose(ps[:, m % 2, b * P:(b + 1) * P], xT[:, m, b * P:(b + 1) * P], ident)
                last.then_inc(y_turned, 1)

            ffn(1, U_FFN2, 2, lambda m: y_turn(m - 2) if m > 1 else None)
            y_turn(DT - 2)
            y_turn(DT - 1)


def dilated_plan(b):
    g2 = [((7 - b + k) * P, 2, k) for k in range(b + 1)]
    g0 = [(G0_AT + (k - b + 1) * P, 0, k) for k in range(max(b - 1, 0), b + 1)]
    g1 = [(G1_AT + i * P, 1, b - i) for i in range(min(b, 4) + 1)]
    end = G1_AT + (min(b, 4) + 1) * P
    segs = [((7 - b) * P, end)] if b else [(7 * P, 8 * P), (9 * P, end)]
    return segs, g2 + g0 + g1


def dilated_windows():
    back = TOE - 1 - P
    return ([(2, G2_AT, 8 * P, back - 7 * P), (0, G0_AT, 2 * P, back - P)]
            + [(1, G1_AT + i * P, P, back - i * P) for i in range(5)])


def t5_bucket(dist):
    exact, last, farthest = 16, 31, 2048
    if dist < exact:
        return dist
    f = np.float32
    large = exact + int(f(np.log(f(dist) / f(exact))) / f(np.log(farthest / exact)) * f(exact))
    return min(large, last)


def bias_onehot():
    t = np.zeros((33, NG, TOE), np.float32)
    for g, (w, d) in enumerate(DIL):
        for x in range(TOE):
            dist = S - 1 - x
            ok = 0 <= dist <= w and dist % d == 0
            t[t5_bucket(dist) if ok else 32, g, x] = 1.0
    return t.reshape(33, NG * TOE)


def constants():
    i, j = np.arange(P)[:, None], np.arange(P)[None, :]
    one = np.ones((P, P))
    tiles = [i == j, -1.0 * (i >= j), -one, one, i // HD == j // HD, i < j, NEG * (i >= j)]
    return np.ascontiguousarray(np.stack([np.asarray(t, np.float32) for t in tiles], axis=1))


def column_units(w, tiles):
    n = w.shape[0] // P
    return [w[:, c * P:(c + 1) * P].reshape(n, P, P).transpose(1, 0, 2).reshape(P, n * P) for c in tiles]


def swiglu_units(w_gu, w_down):
    def gu(g):
        return column_units(w_gu, [c for t in range(GT * g, GT * g + GT) for c in (t, FT + t)])

    def down(g):
        return [w_down[f * P:(f + 1) * P] for f in range(GT * g, GT * g + GT)]

    units = gu(0)
    for g in range(1, NGRP):
        units += gu(g) + down(g - 1)
    return units + down(NGRP - 1)


def weight_units(w_mem_kv, f1_gu, f1_down, w_in, w_br, w_out, f2_gu, f2_down):
    units = column_units(w_mem_kv, range(4)) + swiglu_units(f1_gu, f1_down)
    units += column_units(w_in, [q + 3 * i for q in range(3) for i in range(3)])
    units += column_units(w_in, [18, 19] + list(range(9, 18)))
    for m in range(DT):
        units += column_units(w_in, [20 + b * DT + m for b in range(3)])
        units += [np.pad(column_units(w_br, [m])[0], ((0, 0), (0, (DT - BR) * P)))]
    units += column_units(w_out, range(DT)) + swiglu_units(f2_gu, f2_down)
    return np.ascontiguousarray(np.stack(units))


_ORDER = ["x", "mem", "weights", "gains", "head_gains", "rel_bias", "consts", "onehot"]


def kernel(**inputs):
    import concourse.bacc as _bacc
    from concourse.bass_utils import run_bass_kernel_spmd as _run

    a = {k: np.asarray(v) for k, v in inputs.items()}
    w_br = np.concatenate([a["w_br_sb"][0], a["w_br_dil"][0], a["w_br_x"][0]], axis=0)
    arrays = {
        "x": a["x"][0],
        "mem": a["mem"][0],
        "weights": weight_units(a["w_mem_kv"][0], a["ffn1_w_gu"][0], a["ffn1_w_down"][0], a["w_in"][0], w_br,
                                a["w_out"][0], a["ffn2_w_gu"][0], a["ffn2_w_down"][0]),
        "gains": np.stack([a[n][0].reshape(DT, P).T for n in ("ffn1_norm", "mix_norm", "ffn2_norm", "mem_norm")], axis=1),
        "head_gains": np.stack([np.tile(a[n][0], 2) for n in ("dil_q_gain", "dil_k_gain", "x_q_gain", "x_k_gain")], axis=1),
        "rel_bias": a["rel_bias"],
        "consts": constants(),
        "onehot": bias_onehot(),
    }
    nc = _bacc.Bacc("TRN2", target_bir_lowering=False, num_devices=1)
    arrays = {f"in_{n}": np.ascontiguousarray(v) for n, v in arrays.items()}
    args = [nc.dram_tensor(f"in_{n}", arrays[f"in_{n}"].shape, F32, kind="ExternalInput").ap() for n in _ORDER]
    out = nc.dram_tensor("out_0", (S, D), F32, kind="ExternalOutput").ap()
    layer(nc, *args, out)
    r = _run(nc, [arrays], core_ids=[0])
    return r.results[0]["out_0"].reshape(1, S, D)
```
